# Optimizing a Trainium2 kernel written in Bass

```python
import jax, jax.numpy as jnp
from jax import lax
import numpy as np

D_MODEL = 1024
BATCH = 1
SEQ = 256
DEPTH = 1

SC_WIDTH = D_MODEL
CONV_K = 3
GMLP_WIDTH = D_MODEL
GMLP_GROUPS = 8
GMLP_GROUP_DIM = GMLP_WIDTH // GMLP_GROUPS
CHUNK = 128
N_EXPERTS = 32
TOP_K = 4
D_FF = D_MODEL
SWIGLU_LIMIT = 7.0
SWIGLU_ALPHA = 1.702
MOE_BLOCK = 256
NORM_EPS = 1e-6
D_IN = 3 * SC_WIDTH + 2 * GMLP_WIDTH + 2 * D_MODEL

kernel_name = "hybrid_conv_gmlp_moe_adaln_trunk"

def rms_norm(x, g):
    xf = x.astype(jnp.float32)
    y = xf * lax.rsqrt(jnp.mean(xf * xf, axis=-1, keepdims=True) + NORM_EPS)
    return (y * g.astype(jnp.float32)).astype(x.dtype)

def layer_norm(x, g):
    xf = x.astype(jnp.float32)
    mu = jnp.mean(xf, axis=-1, keepdims=True)
    xc = xf - mu
    var = jnp.mean(xc * xc, axis=-1, keepdims=True)
    return (xc * lax.rsqrt(var + NORM_EPS) * g.astype(jnp.float32)).astype(x.dtype)

def modulate(h, shift, scale):
    return h * (1 + scale) + shift

def causal_dwconv3(z, w):
    z1 = jnp.pad(z, ((0, 0), (1, 0), (0, 0)))[:, :-1]
    z2 = jnp.pad(z, ((0, 0), (2, 0), (0, 0)))[:, :-2]
    return w[0] * z2 + w[1] * z1 + w[2] * z

def chunked_spatial_gate(u, v, w_s, b_s):
    bsz, seq, _ = v.shape
    vc = v.reshape(bsz, seq // CHUNK, CHUNK, GMLP_GROUPS, GMLP_GROUP_DIM)
    mask = jnp.tril(jnp.ones((CHUNK, CHUNK), dtype=w_s.dtype))
    s = jnp.einsum("gts,bnsgc->bntgc", w_s * mask, vc) + b_s.T[:, :, None]
    return u * s.reshape(bsz, seq, GMLP_WIDTH)

def hybrid_mixer(h, w_in, conv_w, w_s, b_s, ln_v_g, w_out):
    z = h @ w_in
    o1 = SC_WIDTH
    o2 = 2 * SC_WIDTH
    o3 = 3 * SC_WIDTH
    o4 = o3 + GMLP_WIDTH
    o5 = o4 + GMLP_WIDTH
    o6 = o5 + D_MODEL
    sc_x, sc_b, sc_c = z[..., :o1], z[..., o1:o2], z[..., o2:o3]
    u, v = z[..., o3:o4], z[..., o4:o5]
    gate_a, gate_b = z[..., o5:o6], z[..., o6:]
    y_a = sc_b * causal_dwconv3(sc_c * sc_x, conv_w)
    u = jax.nn.gelu(u, approximate=False)
    v = layer_norm(jax.nn.gelu(v, approximate=False), ln_v_g)
    y_b = chunked_spatial_gate(u, v, w_s, b_s)
    m = jax.nn.sigmoid(gate_a) * y_a + jax.nn.sigmoid(gate_b) * y_b
    return m @ w_out

def moe_ffn(h, router_w, router_b, w_gu, b_gu, w_dn, b_dn):
    n_tok, d = h.shape
    logits = (h @ router_w + router_b).astype(jnp.float32)
    top_logit, top_e = lax.top_k(logits, TOP_K)
    top_w = jax.nn.softmax(top_logit, axis=-1)
    n_assign = n_tok * TOP_K
    flat_e = top_e.reshape(-1)
    order = jnp.argsort(flat_e)
    sorted_e = flat_e[order]
    sorted_tok = order // TOP_K
    sorted_w = top_w.reshape(-1)[order].astype(h.dtype)
    counts = jnp.bincount(flat_e, length=N_EXPERTS)
    padded = (counts + MOE_BLOCK - 1) // MOE_BLOCK * MOE_BLOCK
    pad_end = jnp.cumsum(padded)
    pad_start = pad_end - padded
    grp_start = jnp.cumsum(counts) - counts
    dest = pad_start[sorted_e] + (jnp.arange(n_assign) - grp_start[sorted_e])
    n_blocks = -(-n_assign // MOE_BLOCK) + N_EXPERTS
    row_tok = jnp.zeros((n_blocks * MOE_BLOCK,), jnp.int32).at[dest].set(sorted_tok)
    block_e = jnp.minimum(
        jnp.searchsorted(pad_end, jnp.arange(n_blocks) * MOE_BLOCK, side="right"), N_EXPERTS - 1)
    xb = h[row_tok].reshape(n_blocks, MOE_BLOCK, d)

    def expert_block(args):
        xs, e = args
        gu = xs @ w_gu[e] + b_gu[e]
        gate, up = gu[:, :D_FF], gu[:, D_FF:]
        gate = jnp.minimum(gate, SWIGLU_LIMIT)
        up = jnp.clip(up, -SWIGLU_LIMIT, SWIGLU_LIMIT)
        act = gate * jax.nn.sigmoid(SWIGLU_ALPHA * gate) * (up + 1)
        return act @ w_dn[e] + b_dn[e]

    yb = lax.map(expert_block, (xb, block_e)).reshape(-1, d)
    y_sorted = yb[dest] * sorted_w[:, None]
    return jax.ops.segment_sum(y_sorted, sorted_tok, num_segments=n_tok)

def setup_inputs(seed: int = 0) -> dict:
    key = jax.random.key(seed)
    ks = jax.random.split(key, 19)

    def nrm(k, shape, std):
        return jax.random.normal(k, shape, jnp.float32) * std

    return {
        "x": nrm(ks[0], (BATCH, SEQ, D_MODEL), 1.0),
        "c": nrm(ks[1], (BATCH, D_MODEL), 1.0),
        "w_ada": nrm(ks[2], (DEPTH, D_MODEL, 6 * D_MODEL), 0.5 * D_MODEL ** -0.5),
        "b_ada": nrm(ks[3], (DEPTH, 6 * D_MODEL), 0.1),
        "norm_mix_g": 1.0 + nrm(ks[4], (DEPTH, D_MODEL), 0.05),
        "w_in": nrm(ks[5], (DEPTH, D_MODEL, D_IN), D_MODEL ** -0.5),
        "conv_w": nrm(ks[6], (DEPTH, CONV_K, SC_WIDTH), CONV_K ** -0.5),
        "w_spatial": nrm(ks[7], (DEPTH, GMLP_GROUPS, CHUNK, CHUNK), CHUNK ** -0.5),
        "b_spatial": 1.0 + nrm(ks[8], (DEPTH, GMLP_GROUPS, CHUNK), 0.1),
        "ln_v_g": 1.0 + nrm(ks[9], (DEPTH, GMLP_WIDTH), 0.05),
        "w_out": nrm(ks[10], (DEPTH, D_MODEL, D_MODEL), D_MODEL ** -0.5),
        "norm_ffn_g": 1.0 + nrm(ks[11], (DEPTH, D_MODEL), 0.05),
        "router_w": nrm(ks[12], (DEPTH, D_MODEL, N_EXPERTS), D_MODEL ** -0.5),
        "router_b": nrm(ks[13], (DEPTH, N_EXPERTS), 0.01),
        "w_gate_up": nrm(ks[14], (DEPTH, N_EXPERTS, D_MODEL, 2 * D_FF), D_MODEL ** -0.5),
        "b_gate_up": nrm(ks[15], (DEPTH, N_EXPERTS, 2 * D_FF), 0.02),
        "w_down": nrm(ks[16], (DEPTH, N_EXPERTS, D_FF, D_MODEL), D_FF ** -0.5),
        "b_down": nrm(ks[17], (DEPTH, N_EXPERTS, D_MODEL), 0.02),
        "final_norm_g": 1.0 + nrm(ks[18], (D_MODEL,), 0.05),
    }

def reference(x, c, w_ada, b_ada, norm_mix_g, w_in, conv_w, w_spatial, b_spatial, ln_v_g,
              w_out, norm_ffn_g, router_w, router_b, w_gate_up, b_gate_up, w_down, b_down,
              final_norm_g):
    bsz, seq, d = x.shape
    cond = jax.nn.silu(c)
    for l in range(DEPTH):
        mod = (cond @ w_ada[l] + b_ada[l])[:, None, :]
        sh_m, sc_m, g_m, sh_f, sc_f, g_f = jnp.split(mod, 6, axis=-1)
        h = modulate(rms_norm(x, norm_mix_g[l]), sh_m, sc_m)
        x = x + g_m * hybrid_mixer(h, w_in[l], conv_w[l], w_spatial[l], b_spatial[l],
                                   ln_v_g[l], w_out[l])
        h = modulate(rms_norm(x, norm_ffn_g[l]), sh_f, sc_f)
        y = moe_ffn(h.reshape(-1, d), router_w[l], router_b[l], w_gate_up[l], b_gate_up[l],
                    w_down[l], b_down[l])
        x = x + g_f * y.reshape(bsz, seq, d)
    return rms_norm(x, final_norm_g)


_drawn_inputs = setup_inputs


def setup_inputs(seed=0):
    import zlib

    import numpy as np

    out = dict(_drawn_inputs(seed))
    spreads = {}
    factors = {'b_spatial': 3.601, 'ln_v_g': 6.097, 'router_b': 11.754, 'b_gate_up': 8.0, 'b_down': 8.0}
    for name, (base, spread) in spreads.items():
        noise = np.random.default_rng([zlib.crc32(name.encode()), seed]).standard_normal(out[name].shape)
        drawn = base * np.exp(spread * noise) if base else spread * noise
        out[name] = __import__('jax').numpy.asarray(drawn.astype(out[name].dtype))
    for name, factor in factors.items():
        out[name] = (out[name] * factor).astype(out[name].dtype)
    return out
```

```python
import concourse.bass as bass
from concourse import mybir
from contextlib import ExitStack


def hybrid_trunk(nc, x_in, c_in, w_ada, b_ada, norm_mix_g, w_in, conv_w, w_spatial, b_spatial, ln_v_g,
                 w_out, norm_ffn_g, router_w, router_b, w_gate_up, b_gate_up, w_down, b_down,
                 final_norm_g, out):
    f32, i32, u32 = mybir.dt.float32, mybir.dt.int32, mybir.dt.uint32
    ALU, ACT, AX = mybir.AluOpType, mybir.ActivationFunctionType, mybir.AxisListType
    ds = bass.ds

    P = 128
    DEPTH, D, D_IN = w_in.shape
    T = x_in.shape[1]
    E = router_w.shape[2]
    FF = w_down.shape[2]
    NG = w_spatial.shape[1]
    TOP_K = 4
    LIMIT, ALPHA, EPS = 7.0, 1.702, 1e-6
    TA = T // P
    KT = D // P
    HALF = 512
    NH = D // HALF
    CAP = 64
    MAXR = T // CAP
    QW = HALF // P
    assert DEPTH == 1 and T == 2 * P and D == 2 * HALF and FF == D and NG == KT and E == 32

    SC_X, SC_B, SC_C, U_, V_, GATE_A, GATE_B = range(7)
    SECTIONS = [SC_C, SC_X, SC_B, GATE_A, U_, GATE_B]
    NS = len(SECTIONS)

    UW = KT * HALF
    RING = 8
    SLOTS = 10
    units = [("ada", 0, q) for q in range(4)] + [("in", V_, h) for h in range(NH)]
    for h in range(NH):
        units += [("in", s, h) for s in SECTIONS]
        units += [("ada", 1 + h, q) for q in range(4)]
    units += [("out", 0, h) for h in range(NH)]
    unit_no = {u: n for n, u in enumerate(units)}
    NU = len(units)

    ctx = ExitStack()
    with ctx:
        def sb(name, shape, dt=f32):
            return ctx.enter_context(nc.sbuf_tensor(name, shape, dt))

        def sem(name):
            return ctx.enter_context(nc.semaphore(name))

        W = sb("W", [P, SLOTS * UW])
        x_sb = sb("x_sb", [P, TA, D])
        HV = sb("HV", [P, TA, D])
        hT = sb("hT", [P, KT, T])
        mT = sb("mT", [P, KT, T])
        mod = sb("mod", [P, 3, HALF])
        EW = sb("EW", [P, 3 * HALF])
        b_gu = sb("b_gu", [P, HALF])
        ident = sb("ident", [P, P])
        iota = sb("iota", [P, CAP])
        pos = sb("pos", [P, TA, E])
        wts = sb("wts", [P, TA, E])
        cols = sb("cols", [P, 5 * KT])
        stat = sb("stat", [P, 64])
        rounds = sb("rounds", [1, E], i32)

        def slot(n, k=1):
            return W[:, n * UW:(n + k) * UW]

        tmp = W[:, RING * UW:SLOTS * UW]
        accA = tmp[:, 0:D].rearrange("p (t n) -> p t n", n=T)
        accB = tmp[:, D:2 * D].rearrange("p (t n) -> p t n", n=T)
        accC = tmp[:, 2 * D:3 * D].rearrange("p (t n) -> p t n", n=T)
        ws_nat = tmp[:, 0:D].rearrange("p (g s) -> p g s", g=NG)
        bs_all = tmp[:, 3 * D:4 * D].rearrange("p (g t) -> p g t", g=NG)
        wsT = tmp[:, 4 * D:5 * D].rearrange("p (g t) -> p g t", g=NG)
        lng = tmp[:, 5 * D:6 * D]
        late = tmp[:, 6 * D:8 * D]
        below = late[:, 0:P]
        ones = late[:, P:2 * P]
        first = late[:, 2 * P:3 * P]
        rw = late[:, 3 * P:3 * P + KT * E].rearrange("p (k e) -> p k e", k=KT)
        cond = late[:, 5 * P:5 * P + KT * 32].rearrange("p (k r) -> p k r", k=KT)
        stack = late[:, 7 * P:7 * P + E]
        rb = late[:, 7 * P + E:7 * P + 2 * E]
        cT = late[:, 7 * P + 2 * E:7 * P + 2 * E + KT]
        shm = late[:, 7 * P + 2 * E + KT:7 * P + 2 * E + 2 * KT]
        scm = late[:, 7 * P + 2 * E + 2 * KT:7 * P + 2 * E + 3 * KT]
        sig = late[:, 8 * P:8 * P + HALF]
        stmp = late[:, 8 * P + HALF:8 * P + 2 * HALF]
        junk = [tmp[:, D:2 * D], tmp[:, 2 * D:3 * D]]
        rows = EW[0:5 * KT, HALF:HALF + P]
        gffn = EW[0:64, 2 * HALF:3 * HALF]
        b_dn = EW[0:E, 0:2 * HALF]
        part = EW[:, 2 * HALF:2 * HALF + T]
        wT = EW[0:E, 2 * HALF + T:2 * HALF + 2 * T]
        onehot = mod[:, 0, 0:8 * E].rearrange("p (n e) -> p n e", e=E)
        logits = mod[:, 0, 8 * E:10 * E].rearrange("p (a e) -> p a e", a=TA)
        mask = mod[:, 0, 10 * E:12 * E].rearrange("p (a e) -> p a e", a=TA)
        top = mod[:, 0, 12 * E:12 * E + 16].rearrange("p (a j) -> p a j", a=TA)
        topi = mod[:, 0, 12 * E + 16:12 * E + 32].bitcast(u32).rearrange("p (a j) -> p a j", a=TA)
        topf = mod[:, 0, 12 * E + 32:12 * E + 48].rearrange("p (a j) -> p a j", a=TA)
        topw = mod[:, 0, 12 * E + 48:12 * E + 56].rearrange("p (a j) -> p a j", a=TA)
        negm = mod[:, 0, 12 * E + 56:12 * E + 58]
        esum = mod[:, 0, 12 * E + 58:12 * E + 60]
        cnt = [mod[0:1, 0, 12 * E + 64:13 * E + 64], mod[0:1, 0, 13 * E + 64:14 * E + 64]]

        def w_half(n, rows_):
            return slot(n, 2).rearrange("p (k n) -> p k n", k=KT)[:, rows_, :]

        GATE_SLOT, UP_SLOT, DOWN_SLOT = (4, 0), (6, 2), 8
        work = mT[:, :, :].rearrange("p k t -> p (k t)")
        S = work[:, 0:256].rearrange("p (a s) -> p a s", a=TA)
        Sw = work[:, 256:512].rearrange("p (a s) -> p a s", a=TA)
        SwT = [work[:, 512 + 256 * r:768 + 256 * r] for r in range(2)]
        hg = work[:, 1024:1536]
        hTg = work[:, 1536:2048].rearrange("p (q s) -> p q s", q=QW)
        work2 = hT[:, :, :].rearrange("p k t -> p (k t)")
        sel = [work2[:, 256 * r:256 * (r + 1)].rearrange("p (j s) -> p j s", j=4) for r in range(2)]
        actT = work2[:, 512:1024].rearrange("p (q s) -> p q s", q=QW)
        y = work2[:, 1024:1536]
        yx = work2[:, 1536:2048]
        hTx = mod[:, 0, :].rearrange("p (q s) -> p q s", q=QW)
        SwTx = mod[:, 1, 0:256]
        kept = mod[:, 1, 256:256 + P]
        gs, sg, ua = EW[:, 0:HALF], EW[:, HALF:2 * HALF], EW[:, 2 * HALF:3 * HALF]

        B = [ctx.enter_context(nc.psum_tensor(f"B{n}", [P, HALF], f32)) for n in range(8)]
        Yb = [[B[2 * a + g] for g in range(NH)] for a in range(TA)]
        G, Ub, Db, Xb = B[4], B[5], B[6], B[7]

        s_x = sem("s_x"); s_rows = sem("s_rows"); s_bada = sem("s_bada"); s_gffn = sem("s_gffn")
        s_ws = sem("s_ws"); s_bs = sem("s_bs"); s_lng = sem("s_lng"); s_rw = sem("s_rw")
        s_bgu = sem("s_bgu"); s_bdn = sem("s_bdn"); s_gfin = sem("s_gfin"); s_out = sem("s_out")
        s_slot = [sem(f"s_slot{n}") for n in range(RING)]
        unit_used = sem("unit_used")
        c_ident = sem("c_ident"); c_iota = sem("c_iota"); c_late = sem("c_late"); pool_step = sem("pool_step")
        ws_masked = sem("ws_masked"); first_kept = sem("first_kept")
        dve_step = sem("dve_step")
        act_step = sem("act_step")
        x_sq = sem("x_sq"); x_var = sem("x_var"); x_std = sem("x_std"); xn_ready = sem("xn_ready")
        xnT_done = sem("xnT_done"); rowsT_done = sem("rowsT_done"); cols_ready = sem("cols_ready")
        silu_done = sem("silu_done"); cond_ready = sem("cond_ready")
        ada_done = sem("ada_done"); mod_ready = sem("mod_ready"); modT_done = sem("modT_done")
        scale_ready = sem("scale_ready"); hT_act = sem("hT_act"); hT_dve = sem("hT_dve")
        wsT_done = sem("wsT_done"); wsT_ready = sem("wsT_ready")
        v_done = sem("v_done"); v_gelu = sem("v_gelu"); v_mu = sem("v_mu"); v_sq = sem("v_sq")
        v_var = sem("v_var"); v_std = sem("v_std"); v_ready = sem("v_ready")
        sec_done = sem("sec_done")
        sec_act = sem("sec_act")
        sec_dve = sem("sec_dve")
        sp_done = sem("sp_done"); sp_used = sem("sp_used"); m_ready = sem("m_ready")
        mix_done = sem("mix_done"); gm_done = sem("gm_done"); gm_sb = sem("gm_sb")
        x2_ready = sem("x2_ready"); x2_sq = sem("x2_sq"); x2_var = sem("x2_var"); x2_std = sem("x2_std")
        fs_row = sem("fs_row"); fs_done = sem("fs_done"); fh_done = sem("fh_done")
        h2_ready = sem("h2_ready"); h2T_done = sem("h2T_done"); h2T_act = sem("h2T_act"); h2T_dve = sem("h2T_dve")
        part_done = sem("part_done"); part_ready = sem("part_ready"); lg_done = sem("lg_done")
        top_ready = sem("top_ready"); exp_done = sem("exp_done"); mask_ready = sem("mask_ready")
        wts_ready = sem("wts_ready"); rank_done = sem("rank_done"); wT_done = sem("wT_done")
        wT_ready = sem("wT_ready"); table_ready = sem("table_ready"); swT_zero = sem("swT_zero")
        y_open = sem("y_open")
        s_gate = [[sem(f"s_gate{r}{q}") for q in range(4)] for r in range(2)]
        s_up = [[sem(f"s_up{r}{q}") for q in range(4)] for r in range(2)]
        s_down = [sem(f"s_down{q}") for q in range(4)]
        s_ready = sem("s_ready"); sw_ready = sem("sw_ready"); sel_ready = sem("sel_ready")
        gathered = sem("gathered"); hg_ready = sem("hg_ready"); hTg_done = sem("hTg_done")
        hTg_ready = sem("hTg_ready"); gate_done = sem("gate_done"); gmin_ready = sem("gmin_ready")
        sig_ready = sem("sig_ready"); gs_ready = sem("gs_ready"); swT_done = sem("swT_done")
        swT_ready = sem("swT_ready"); up_done = sem("up_done"); clip_done = sem("clip_done")
        act_ready = sem("act_ready"); actT_done = sem("actT_done"); actT_ready = sem("actT_ready")
        down_done = sem("down_done"); y_ready = sem("y_ready"); passed = sem("passed")
        x_s = sem("x_s"); x_gath = sem("x_gath"); x_hg = sem("x_hg")
        x_hTd = sem("x_hTd"); x_hT = sem("x_hT"); x_sw = sem("x_sw"); x_gate = sem("x_gate")
        x_gmin = sem("x_gmin"); x_sig = sem("x_sig"); x_gs = sem("x_gs"); x_up = sem("x_up")
        x_clip = sem("x_clip"); x_act = sem("x_act"); x_actTd = sem("x_actTd"); x_actT = sem("x_actT")
        x_down = sem("x_down"); x_y = sem("x_y"); x_swTd = sem("x_swTd"); x_swT = sem("x_swT")
        x_end = sem("x_end")
        y_all = sem("y_all"); gf_done = sem("gf_done"); gf_sb = sem("gf_sb"); x3_ready = sem("x3_ready")
        x3_sq = sem("x3_sq"); x3_var = sem("x3_var"); x3_std = sem("x3_std"); o_ready = sem("o_ready")

        ada_v = w_ada[0].rearrange("(q k p) n -> q p k n", k=2, p=P)
        in_v = w_in[0].rearrange("(k p) n -> p k n", p=P)
        out_v = w_out[0].rearrange("(k p) n -> p k n", p=P)
        gu_v = w_gate_up[0].rearrange("e (q k p) n -> e q p k n", k=2, p=P)
        dn_v = w_down[0].rearrange("e (q k p) n -> e q p k n", k=2, p=P)

        SS, VAR, STD, RST = 0, 4, 6, 8
        VS, NMU, VSS, VVAR, VSTD, VRST = 10, 14, 16, 18, 20, 22
        SS2, VAR2, STD2, RST2 = 24, 30, 32, 34
        SS3, VAR3, STD3, RST3 = 36, 42, 44, 46

        dve_order = [(h, s, b) for h in range(NH) for s in SECTIONS if s not in (SC_C, U_) for b in range(2)]

        def dve_bank(h, s, b):
            return dve_order.index((h, s, b)) + 1

        act_order = [(h, s, b) for h in range(NH) for s in SECTIONS if s in (SC_C, GATE_A, U_, GATE_B) for b in range(2)]

        def act_bank(h, s, b):
            return act_order.index((h, s, b)) + 1

        block = ctx.enter_context(nc.Block())

        @block.sync
        def _(sp):
            for n, (kind, s, h) in enumerate(units):
                if n >= RING:
                    sp.wait_ge(unit_used, n - RING + 1)
                if kind == "ada":
                    src = ada_v[h, :, :, 4 * HALF * s:4 * HALF * (s + 1)]
                    dst = slot(n % RING).rearrange("p (k n) -> p k n", k=2)
                else:
                    c0 = (s * D if kind == "in" else 0) + h * HALF
                    src = (in_v if kind == "in" else out_v)[:, :, c0:c0 + HALF]
                    dst = slot(n % RING).rearrange("p (k n) -> p k n", k=KT)
                sp.dma_start(dst, src).then_inc(s_slot[n % RING], 16)

            def load_gate_up(e, r):
                for q in range(4):
                    sp.dma_start(w_half(GATE_SLOT[r], slice(2 * q, 2 * q + 2)),
                                 gu_v[e, q, :, :, 0:FF]).then_inc(s_gate[r][q], 16)
                for q in range(4):
                    sp.dma_start(w_half(UP_SLOT[r], slice(2 * q, 2 * q + 2)),
                                 gu_v[e, q, :, :, FF:2 * FF]).then_inc(s_up[r][q], 16)

            def load_down(e, qs):
                for q in qs:
                    sp.dma_start(w_half(DOWN_SLOT, slice(2 * q, 2 * q + 2)),
                                 dn_v[e, q, :, :, :]).then_inc(s_down[q], 16)

            sp.wait_ge(unit_used, NU - RING + 4)
            load_gate_up(0, 0)
            sp.wait_ge(m_ready, NH * NH)
            load_down(0, (0, 1, 2))
            sp.wait_ge(unit_used, NU)
            load_gate_up(1, 1)
            sp.wait_ge(table_ready, 1)
            sp.wait_ge(first_kept, 1)
            load_down(0, (3,))
            sp.wait_ge(passed, 1)
            load_down(1, range(4))
            with sp.Fori(1, E // 2) as i:
                for r in range(2):
                    e = 2 * i + r
                    sp.wait_ge(passed, e - 1)
                    load_gate_up(e, r)
                    sp.wait_ge(passed, e)
                    load_down(e, range(4))
            sp.wait_ge(passed, E - 1)
            sp.dma_start(slot(GATE_SLOT[0])[:, 0:D], final_norm_g[:].partition_broadcast(P)).then_inc(s_gfin, 16)
            for a in range(TA):
                sp.wait_ge(o_ready, NH * (a + 1))
                sp.dma_start(out[0, a * P:(a + 1) * P, :], x_sb[:, a, :]).then_inc(s_out, 16)
            sp.wait_ge(s_out, 16 * TA)

        @block.gpsimd
        def _(pool):
            done = [0]

            def one(ins, signal):
                ins.then_inc(pool_step, 1)
                done[0] += 1
                pool.wait_ge(pool_step, done[0])
                if signal is not None:
                    pool.nop().then_inc(signal, 1)

            G_ = nc.gpsimd
            one(G_.memset(ident[:, :], 0.0), None)
            one(G_.affine_select(out=ident[:, :], in_=ident[:, :], compare_op=ALU.not_equal, fill=1.0,
                                 base=0, pattern=[[-1, P]], channel_multiplier=1), c_ident)
            one(G_.iota(iota[:, :], pattern=[[1, CAP]], base=0, channel_multiplier=0,
                        allow_small_or_imprecise_dtypes=True), c_iota)
            pool.wait_ge(s_ws, 16)
            one(G_.affine_select(out=ws_nat, in_=ws_nat, compare_op=ALU.is_ge, fill=0.0,
                                 base=0, pattern=[[0, NG], [-1, P]], channel_multiplier=1), ws_masked)
            one(G_.memset(below, 1.0), None)
            one(G_.affine_select(out=below, in_=below, compare_op=ALU.is_gt, fill=0.0,
                                 base=0, pattern=[[1, P]], channel_multiplier=-1), None)
            one(G_.memset(ones, 1.0), None)
            one(G_.memset(first, 0.0), None)
            one(G_.memset(stack, 0.0), None)
            for j in range(4):
                v = stack[32 * j:32 * j + 32, :]
                one(G_.affine_select(out=v, in_=v, compare_op=ALU.not_equal, fill=1.0,
                                     base=0, pattern=[[-1, E]], channel_multiplier=1), None)
                one(G_.memset(first[32 * j:32 * j + 1, :], 1.0), c_late if j == 3 else None)
            pool.wait_ge(lg_done, 1)
            one(G_.memset(y, 0.0), y_ready)
            one(G_.memset(SwT[1], 0.0), swT_zero)
            one(G_.tensor_copy(kept, first), first_kept)

        @block.scalar
        def _(act):
            A = nc.scalar.activation
            act.dma_start(x_sb[:, :, :], x_in[0].rearrange("(a p) n -> p a n", p=P)).then_inc(s_x, 16)
            act.dma_start(rows[0:KT, :], norm_mix_g[0].rearrange("(k p) -> k p", p=P)).then_inc(s_rows, 16)
            act.dma_start(rows[KT:4 * KT, :], conv_w[0].rearrange("j (k p) -> (j k) p", p=P)).then_inc(s_rows, 16)
            act.dma_start(rows[4 * KT:5 * KT, :], c_in[0].rearrange("(k p) -> k p", p=P)).then_inc(s_rows, 16)
            ba = b_ada[0].rearrange("(i j n) -> j i n", i=3, j=4)
            for j in range(4):
                act.dma_start(mod[32 * j:32 * j + 32, :, :], ba[j].partition_broadcast(32)).then_inc(s_bada, 16)
            act.dma_start(ws_nat, w_spatial[0].rearrange("g t s -> t g s")).then_inc(s_ws, 16)
            act.dma_start(bs_all, b_spatial[0].partition_broadcast(P)).then_inc(s_bs, 16)
            act.dma_start(lng, ln_v_g[0].partition_broadcast(P)).then_inc(s_lng, 16)
            gf = norm_ffn_g[0].rearrange("(j n) -> j n", j=NH)
            for j in range(NH):
                act.dma_start(gffn[32 * j:32 * j + 32, :], gf[j].partition_broadcast(32)).then_inc(s_gffn, 16)
            act.dma_start(rw, router_w[0].rearrange("(k p) e -> p k e", p=P)).then_inc(s_rw, 16)
            act.dma_start(rb, router_b[0].partition_broadcast(P)).then_inc(s_rw, 16)
            act.dma_start(b_gu[:, :], b_gate_up[0].rearrange("e (j n) -> (e j) n", j=4)).then_inc(s_bgu, 16)

            act.wait_ge(s_x, 16)
            for a in range(TA):
                A(junk[a], x_sb[:, a, :], ACT.Square, accum_out=stat[:, SS + a:SS + a + 1]).then_inc(x_sq, 1)
            act.wait_ge(x_var, 1)
            A(stat[:, STD:STD + TA], stat[:, VAR:VAR + TA], ACT.Sqrt).then_inc(x_std, 1)
            act.wait_ge(cols_ready, 1)
            A(cT, cols[:, 4 * KT:5 * KT], ACT.Silu).then_inc(silu_done, 1)
            act.dma_start(b_dn, b_down[0]).then_inc(s_bdn, 16)
            act.wait_ge(xnT_done, 1)
            act.wait_ge(scale_ready, 1)
            for k in range(KT // 2, KT):
                A(hT[:, k, :], B[k // 2][:, T * (k % 2):T * (k % 2) + T], ACT.Identity,
                  scale=scm[:, k:k + 1], bias=shm[:, k:k + 1]).then_inc(hT_act, 1)
            for h in range(NH):
                for a in range(TA):
                    act.wait_ge(v_done, NH * h + a + 1)
                    A(HV[:, a, h * HALF:(h + 1) * HALF], B[4 + 2 * h + a][:, :], ACT.Gelu,
                      accum_out=stat[:, VS + 2 * a + h:VS + 2 * a + h + 1]).then_inc(v_gelu, 1)
            act.wait_ge(v_mu, 1)
            for a in range(TA):
                A(junk[a], HV[:, a, :], ACT.Square, bias=stat[:, NMU + a:NMU + a + 1],
                  accum_out=stat[:, VSS + a:VSS + a + 1]).then_inc(v_sq, 1)
            act.wait_ge(v_var, 1)
            A(stat[:, VSTD:VSTD + TA], stat[:, VVAR:VVAR + TA], ACT.Sqrt).then_inc(v_std, 1)
            for h in range(NH):
                for n, s in enumerate(SECTIONS):
                    for b in range(2):
                        m = 2 * (NS * h + n) + b
                        bank = B[m % 6][:, :]
                        if s in (SC_X, SC_B):
                            continue
                        act.wait_ge(sec_done, m + 1)
                        if s == SC_C:
                            if h == 0 and b == 0:
                                act.wait_ge(wsT_done, 1)
                            if h > 0:
                                act.wait_ge(m_ready, NH * (h - 1) + b + 1)
                            A(accA[:, 2 * b:2 * b + 2, :], bank.rearrange("p (t n) -> p t n", n=T), ACT.Copy).then_inc(sec_act, 1)
                        elif s == U_:
                            if h > 0:
                                act.wait_ge(m_ready, NH * (h - 1) + b + 1)
                            A(accC[:, 2 * b:2 * b + 2, :], bank.rearrange("p (t n) -> p t n", n=T), ACT.Gelu).then_inc(sec_act, 1)
                        else:
                            if s == GATE_A and b == 0 and h > 0:
                                act.wait_ge(sec_dve, dve_bank(h - 1, GATE_B, 1))
                            if s == GATE_A and b == 1:
                                act.wait_ge(sec_dve, dve_bank(h, GATE_A, 0))
                            if s == GATE_B:
                                act.wait_ge(sec_dve, dve_bank(h, GATE_A, 1) if b == 0 else dve_bank(h, GATE_B, 0))
                            A(sig, bank, ACT.Sigmoid).then_inc(sec_act, 1)
            for h in range(NH):
                act.wait_ge(gm_done, h + 1)
                A(HV[:, 0, h * HALF:(h + 1) * HALF], B[4 + h][:, :], ACT.Copy).then_inc(gm_sb, 1)
            for n in range(TA * NH):
                act.wait_ge(x2_ready, n + 1)
                a, h = n % TA, n // TA
                A(sig if n % 2 else stmp, x_sb[:, a, h * HALF:(h + 1) * HALF], ACT.Square,
                  accum_out=stat[:, SS2 + 2 * a + h:SS2 + 2 * a + h + 1]).then_inc(x2_sq, 1)
                act.wait_ge(x2_sq, n + 1)
            act.wait_ge(x2_var, 1)
            A(stat[:, STD2:STD2 + TA], stat[:, VAR2:VAR2 + TA], ACT.Sqrt).then_inc(x2_std, 1)
            act.wait_ge(h2T_done, 2)
            for b in (2, 3):
                A(hT[:, 2 * b:2 * b + 2, :], B[b][:, :].rearrange("p (k t) -> p k t", t=T), ACT.Copy).then_inc(h2T_act, 1)
            act.wait_ge(top_ready, 1)
            for a in range(TA):
                A(topw[:, a, :], top[:, a, 0:TOP_K], ACT.Exp, bias=negm[:, a:a + 1],
                  accum_out=esum[:, a:a + 1]).then_inc(exp_done, 1)
            act.wait_ge(wT_done, 1)
            A(wT, B[7][0:E, 0:T], ACT.Copy).then_inc(wT_ready, 1)

            act.wait_ge(gathered, 1)
            A(hg, Db[:, :], ACT.Copy).then_inc(hg_ready, 1)
            nx = act.alloc_register("act_rounds")
            act.reg_mov(nx, 0)

            def expert(e, r, last=False):
                act.wait_ge(gmin_ready, e + 1)
                A(sg, gs, ACT.Sigmoid, scale=ALPHA).then_inc(sig_ready, 1)
                act.wait_ge(swT_done, e + 1)
                A(SwT[r], Xb[:, 0:T], ACT.Copy).then_inc(swT_ready, 1)
                if not last:
                    act.wait_ge(gathered, e + 2)
                    A(hg, Db[:, :], ACT.Copy).then_inc(hg_ready, 1)
                act.wait_ge(actT_done, e + 1)
                A(actT, Xb[:, :].rearrange("p (q s) -> p q s", q=QW), ACT.Copy).then_inc(actT_ready, 1)
                act.wait_ge(down_done, e + 1)
                A(y, Db[:, :], ACT.Copy).then_inc(y_ready, 1)
                more = act.value_load(rounds[0:1, ds(e, 1)], min_val=0, max_val=MAXR - 1)
                with act.If(more > 0):
                    with act.Fori(0, more):
                        n = act.snap(nx, min_val=0, max_val=(MAXR - 1) * E)
                        act.wait_ge(x_gath, n + 1)
                        A(hg, Xb[:, :], ACT.Copy).then_inc(x_hg, 1)
                        act.wait_ge(x_gmin, n + 1)
                        A(sg, gs, ACT.Sigmoid, scale=ALPHA).then_inc(x_sig, 1)
                        act.wait_ge(x_actTd, n + 1)
                        A(actT, Xb[:, :].rearrange("p (q s) -> p q s", q=QW), ACT.Copy).then_inc(x_actT, 1)
                        act.wait_ge(x_swTd, n + 1)
                        A(SwTx, Xb[:, 0:T], ACT.Copy).then_inc(x_swT, 1)
                        act.wait_ge(x_down, n + 1)
                        A(yx, Db[:, :], ACT.Copy).then_inc(x_y, 1)
                        act.wait_ge(x_end, n + 1)
                        act.reg_add(nx, nx, 1)

            act.wait_ge(table_ready, 1)
            with act.Fori(0, E // 2 - 1) as i:
                for r in range(2):
                    expert(2 * i + r, r)
            expert(E - 2, 0)
            expert(E - 1, 1, last=True)

            for h in range(NH):
                act.wait_ge(gf_done, h + 1)
                A(HV[:, 0, h * HALF:(h + 1) * HALF], B[4 + h][:, :], ACT.Copy).then_inc(gf_sb, 1)
            for n in range(TA * NH):
                act.wait_ge(x3_ready, n + 1)
                a, h = n // NH, n % NH
                A(sg if n % 2 else gs, x_sb[:, a, h * HALF:(h + 1) * HALF], ACT.Square,
                  accum_out=stat[:, SS3 + 2 * a + h:SS3 + 2 * a + h + 1]).then_inc(x3_sq, 1)
                act.wait_ge(x3_sq, n + 1)
                if n % NH == NH - 1:
                    act.wait_ge(x3_var, a + 1)
                    A(stat[:, STD3 + a:STD3 + a + 1], stat[:, VAR3 + a:VAR3 + a + 1], ACT.Sqrt).then_inc(x3_std, 1)

        @block.vector
        def _(dve):
            V = nc.vector
            steps = [0]

            def step(ins):
                steps[0] += 1
                ins.then_inc(dve_step, 1)
                dve.wait_ge(dve_step, steps[0])

            dve.wait_ge(x_sq, TA)
            V.tensor_scalar(stat[:, VAR:VAR + TA], stat[:, SS:SS + TA], 1.0 / D, EPS, ALU.mult, ALU.add).then_inc(x_var, 1)
            dve.wait_ge(x_std, 1)
            step(V.reciprocal(stat[:, RST:RST + TA], stat[:, STD:STD + TA]))
            for a in range(TA):
                V.tensor_scalar(HV[:, a, :], x_sb[:, a, :], stat[:, RST + a:RST + a + 1], None, ALU.mult).then_inc(xn_ready, 1)
            dve.wait_ge(rowsT_done, 1)
            V.tensor_copy(cols[:, :], B[6][:, 0:5 * KT]).then_inc(cols_ready, 1)
            dve.wait_ge(silu_done, 1)
            V.tensor_copy(cond, cT.unsqueeze(2).broadcast_to([P, KT, 32])).then_inc(cond_ready, 1)
            dve.wait_ge(wsT_done, 1)
            for b in range(2):
                V.tensor_copy(wsT[:, 4 * b:4 * b + 4, :], B[4 + b][:, :].rearrange("p (g t) -> p g t", t=P)).then_inc(wsT_ready, 1)

            def add_bias(i):
                if i == 0:
                    dve.wait_ge(s_bada, 64)
                dve.wait_ge(ada_done, i + 1)
                V.tensor_tensor(mod[:, i, :], B[7][:, :], mod[:, i, :], ALU.add).then_inc(mod_ready, 1)

            add_bias(0)
            dve.wait_ge(modT_done, 1)
            mt = B[7][:, :].rearrange("p (q j r) -> p j q r", q=QW, j=4)
            step(V.tensor_copy(shm.rearrange("p (j q) -> p j q", j=NH), mt[:, 0:2, :, 0]))
            dve.wait_ge(cols_ready, 1)
            V.scalar_tensor_tensor(scm.rearrange("p (j q) -> p j q", j=NH), mt[:, 2:4, :, 0], 1.0,
                                   cols[:, 0:KT].rearrange("p (j q) -> p j q", j=NH), ALU.add, ALU.mult).then_inc(scale_ready, 1)
            dve.wait_ge(scale_ready, 1)
            dve.wait_ge(xnT_done, 1)
            for k in range(KT // 2):
                V.tensor_scalar(hT[:, k, :], B[k // 2][:, T * (k % 2):T * (k % 2) + T],
                                scm[:, k:k + 1], shm[:, k:k + 1], ALU.mult, ALU.add).then_inc(hT_dve, 1)
            dve.wait_ge(v_gelu, TA * NH)
            step(V.tensor_tensor(stat[:, NMU:NMU + TA], stat[:, VS:VS + 4:2], stat[:, VS + 1:VS + 4:2], ALU.add))
            V.tensor_scalar(stat[:, NMU:NMU + TA], stat[:, NMU:NMU + TA], -1.0 / D, None, ALU.mult).then_inc(v_mu, 1)
            dve.wait_ge(v_sq, TA)
            V.tensor_scalar(stat[:, VVAR:VVAR + TA], stat[:, VSS:VSS + TA], 1.0 / D, EPS, ALU.mult, ALU.add).then_inc(v_var, 1)
            dve.wait_ge(v_std, 1)
            step(V.reciprocal(stat[:, VRST:VRST + TA], stat[:, VSTD:VSTD + TA]))
            dve.wait_ge(s_lng, 16)
            for a in range(TA):
                step(V.tensor_scalar(HV[:, a, :], HV[:, a, :], stat[:, NMU + a:NMU + a + 1],
                                     stat[:, VRST + a:VRST + a + 1], ALU.add, ALU.mult))
                V.tensor_tensor(HV[:, a, :], HV[:, a, :], lng, ALU.mult).then_inc(v_ready, 1)

            def tiles(bank):
                return bank[:, :].rearrange("p (t n) -> p t n", n=T)

            dve.wait_ge(s_bs, 16)
            for h in range(NH):
                for n, s in enumerate(SECTIONS):
                    for b in range(2):
                        m = 2 * (NS * h + n) + b
                        bank = tiles(B[m % 6])
                        two = slice(2 * b, 2 * b + 2)
                        if s == SC_X:
                            dve.wait_ge(sec_done, m + 1)
                            dve.wait_ge(sec_act, act_bank(h, SC_C, b))
                            if h > 0:
                                dve.wait_ge(m_ready, NH * h)
                            V.tensor_tensor(accA[:, two, :], accA[:, two, :], bank, ALU.mult).then_inc(sec_dve, 1)
                            dve.wait_ge(sec_dve, dve_bank(h, s, b))
                            for t in (2 * b, 2 * b + 1):
                                k = 4 * h + t
                                w = [cols[:, KT * (1 + j) + k:KT * (1 + j) + k + 1] for j in range(3)]
                                step(V.tensor_scalar(accB[:, t, :], accA[:, t, :], w[2], None, ALU.mult))
                                step(V.scalar_tensor_tensor(accB[:, t, 1:T], accA[:, t, 0:T - 1], w[1], accB[:, t, 1:T], ALU.mult, ALU.add))
                                step(V.scalar_tensor_tensor(accB[:, t, 2:T], accA[:, t, 0:T - 2], w[0], accB[:, t, 2:T], ALU.mult, ALU.add))
                        elif s == SC_B:
                            dve.wait_ge(sec_done, m + 1)
                            V.tensor_tensor(accB[:, two, :], accB[:, two, :], bank, ALU.mult).then_inc(sec_dve, 1)
                            dve.wait_ge(sec_dve, dve_bank(h, s, b))
                        elif s == GATE_A:
                            dve.wait_ge(sec_act, act_bank(h, s, b))
                            V.tensor_tensor(accB[:, two, :], accB[:, two, :], tiles(sig), ALU.mult).then_inc(sec_dve, 1)
                        elif s == U_:
                            c = 2 * h + b
                            dve.wait_ge(sp_done, c + 1)
                            bias = bs_all[:, 4 * h + 2 * b:4 * h + 2 * b + 2, :].unsqueeze(2).broadcast_to([P, 2, TA, P])
                            V.tensor_tensor(stmp.rearrange("p (t a n) -> p t a n", t=2, a=TA),
                                            B[6][:, :].rearrange("p (t a n) -> p t a n", t=2, a=TA), bias, ALU.add).then_inc(sp_used, 1)
                            dve.wait_ge(sp_used, c + 1)
                            dve.wait_ge(sec_act, act_bank(h, s, b))
                            step(V.tensor_tensor(accC[:, two, :], accC[:, two, :], tiles(stmp), ALU.mult))
                        elif s == GATE_B:
                            dve.wait_ge(sec_act, act_bank(h, s, b))
                            V.tensor_tensor(accC[:, two, :], accC[:, two, :], tiles(sig), ALU.mult).then_inc(sec_dve, 1)
                            dve.wait_ge(sec_dve, dve_bank(h, s, b))
                            V.tensor_tensor(mT[:, 4 * h + 2 * b:4 * h + 2 * b + 2, :], accB[:, two, :], accC[:, two, :], ALU.add).then_inc(m_ready, 1)
                if h == 0:
                    add_bias(1)
            add_bias(2)
            dve.wait_ge(s_gffn, 16 * NH)
            dve.wait_ge(mod_ready, 3)
            V.scalar_tensor_tensor(mod[0:64, 2, :], mod[0:64, 2, :], 1.0, gffn, ALU.add, ALU.mult).then_inc(fs_row, 1)
            for n in range(TA * NH):
                a, h = n % TA, n // TA
                cs = slice(h * HALF, (h + 1) * HALF)
                dve.wait_ge(mix_done, n + 1)
                dve.wait_ge(gm_sb, h + 1)
                step(V.tensor_tensor(HV[:, 1, cs], B[n][:, :], HV[:, 0, cs], ALU.mult))
                V.tensor_tensor(x_sb[:, a, cs], x_sb[:, a, cs], HV[:, 1, cs], ALU.add).then_inc(x2_ready, 1)
                dve.wait_ge(x2_ready, n + 1)
            dve.wait_ge(x2_sq, TA * NH)
            step(V.tensor_tensor(stat[:, VAR2:VAR2 + TA], stat[:, SS2:SS2 + 4:2], stat[:, SS2 + 1:SS2 + 4:2], ALU.add))
            V.tensor_scalar(stat[:, VAR2:VAR2 + TA], stat[:, VAR2:VAR2 + TA], 1.0 / D, EPS, ALU.mult, ALU.add).then_inc(x2_var, 1)
            dve.wait_ge(x2_std, 1)
            step(V.reciprocal(stat[:, RST2:RST2 + TA], stat[:, STD2:STD2 + TA]))
            for h in range(NH):
                cs = slice(h * HALF, (h + 1) * HALF)
                dve.wait_ge(fs_done, h + 1)
                dve.wait_ge(fh_done, h + 1)
                for a in range(TA):
                    step(V.scalar_tensor_tensor(HV[:, a, cs], x_sb[:, a, cs], stat[:, RST2 + a:RST2 + a + 1], B[6 + h][:, :], ALU.mult, ALU.mult))
                    V.tensor_tensor(HV[:, a, cs], HV[:, a, cs], B[4 + h][:, :], ALU.add).then_inc(h2_ready, 1)
            dve.wait_ge(h2T_done, 1)
            for b in (0, 1):
                V.tensor_copy(hT[:, 2 * b:2 * b + 2, :], B[b][:, :].rearrange("p (k t) -> p k t", t=T)).then_inc(h2T_dve, 1)
            dve.wait_ge(part_done, 1)
            V.tensor_copy(part, B[4][:, 0:T]).then_inc(part_ready, 1)
            dve.wait_ge(lg_done, 1)
            dve.wait_ge(s_rw, 32)
            step(V.tensor_tensor(logits, B[5][:, 0:TA * E].rearrange("p (a e) -> p a e", a=TA),
                                 rb.unsqueeze(1).broadcast_to([P, TA, E]), ALU.add))
            for a in range(TA):
                step(V.max(top[:, a, :], logits[:, a, :]))
            V.tensor_scalar(negm, top[:, :, 0], -1.0, None, ALU.mult).then_inc(top_ready, 1)
            for a in range(TA):
                step(V.max_index(topi[:, a, :], top[:, a, :], logits[:, a, :]))
            step(V.tensor_copy(topf, topi))
            oh = onehot.rearrange("p (a j) e -> p a j e", a=TA)
            for a in range(TA):
                step(V.tensor_tensor(oh[:, a], iota[:, 0:E].unsqueeze(1).broadcast_to([P, TOP_K, E]),
                                     topf[:, a, 0:TOP_K].unsqueeze(2).broadcast_to([P, TOP_K, E]), ALU.is_equal))
            for a in range(TA):
                V.tensor_reduce(mask[:, a, :], oh[:, a].rearrange("p j e -> p e j"), AX.X, ALU.add).then_inc(mask_ready, 1)
            dve.wait_ge(exp_done, TA)
            dve.wait_ge(mask_ready, TA)
            step(V.reciprocal(esum, esum))
            step(V.tensor_tensor(topw, topw, esum.unsqueeze(2).broadcast_to([P, TA, TOP_K]), ALU.mult))
            for a in range(TA):
                step(V.tensor_tensor(oh[:, a], oh[:, a], topw[:, a, :].unsqueeze(2).broadcast_to([P, TOP_K, E]), ALU.mult))
            for a in range(TA):
                V.tensor_reduce(wts[:, a, :], oh[:, a].rearrange("p j e -> p e j"), AX.X, ALU.add).then_inc(wts_ready, 1)
            dve.wait_ge(rank_done, 1)
            step(V.scalar_tensor_tensor(pos[:, :, :], B[6][:, 0:TA * E].rearrange("p (a e) -> p a e", a=TA), 1.0, mask, ALU.add, ALU.mult))
            step(V.tensor_scalar(pos[:, :, :], pos[:, :, :], -1.0, None, ALU.add))
            dve.wait_ge(wts_ready, TA)

            def select(e, dst, signal):
                for a in range(TA):
                    o = dst[:, a, :].rearrange("p (g s) -> p g s", g=NH)
                    V.tensor_scalar(o, iota[:, :].unsqueeze(1).broadcast_to([P, NH, CAP]),
                                    pos[:, a, ds(e, 1)], None, ALU.is_equal).then_inc(signal, 1)

            def select_weighted(e, signal):
                for a in range(TA):
                    o = Sw[:, a, :].rearrange("p (g s) -> p g s", g=NH)
                    V.tensor_scalar(o, iota[:, :].unsqueeze(1).broadcast_to([P, NH, CAP]),
                                    pos[:, a, ds(e, 1)], wts[:, a, ds(e, 1)], ALU.is_equal, ALU.mult).then_inc(signal, 1)

            def select_bias(e, r):
                V.tensor_copy(sel[r], ident[:, ds(4 * e, 4)].unsqueeze(2).broadcast_to([P, 4, CAP])).then_inc(sel_ready, 1)

            select(0, S, s_ready)
            select_weighted(0, sw_ready)
            select_bias(0, 0)
            top_cnt = B[6][0:1, TA * E:TA * E + E]
            step(V.tensor_scalar(cnt[0], top_cnt, float(CAP), None, ALU.is_gt))
            src = 0
            for m in range(2, MAXR):
                o = cnt[1 - src] if m < MAXR - 1 else rounds[:, :]
                ins = V.scalar_tensor_tensor(o, top_cnt, float(CAP * m), cnt[src], ALU.is_gt, ALU.add)
                if m < MAXR - 1:
                    step(ins)
                else:
                    ins.then_inc(table_ready, 1)
                src = 1 - src
            dve.wait_ge(hTg_done, 1)
            V.tensor_copy(hTg, G[:, :].rearrange("p (q s) -> p q s", q=QW)).then_inc(hTg_ready, 1)
            nx = dve.alloc_register("dve_rounds")
            dve.reg_mov(nx, 0)
            dve.wait_ge(table_ready, 1)

            def expert(e, r, last=False):
                if not last:
                    dve.wait_ge(gathered, e + 1)
                    select(e + 1, S, s_ready)
                dve.wait_ge(gate_done, e + 1)
                V.tensor_scalar(gs, G[:, :], LIMIT, None, ALU.min).then_inc(gmin_ready, 1)
                if not last:
                    dve.wait_ge(swT_done, e + 1)
                    select_weighted(e + 1, sw_ready)
                    select_bias(e + 1, 1 - r)
                dve.wait_ge(sig_ready, e + 1)
                V.tensor_tensor(gs, gs, sg, ALU.mult).then_inc(gs_ready, 1)
                dve.wait_ge(up_done, e + 1)
                hw = HALF // 2
                for c in range(2):
                    V.tensor_scalar(ua[:, c * hw:(c + 1) * hw], Ub[:, c * hw:(c + 1) * hw], LIMIT, -LIMIT, ALU.min, ALU.max).then_inc(clip_done, 1)
                dve.wait_ge(gs_ready, e + 1)
                for c in range(2):
                    cs = slice(c * hw, (c + 1) * hw)
                    dve.wait_ge(clip_done, 2 * e + 1 + c)
                    V.scalar_tensor_tensor(ua[:, cs], ua[:, cs], 1.0, gs[:, cs], ALU.add, ALU.mult).then_inc(act_ready, 1)
                if not last:
                    dve.wait_ge(hTg_done, e + 2)
                    V.tensor_copy(hTg, G[:, :].rearrange("p (q s) -> p q s", q=QW)).then_inc(hTg_ready, 1)
                more = dve.value_load(rounds[0:1, ds(e, 1)], min_val=0, max_val=MAXR - 1)
                with dve.If(more > 0):
                    with dve.Fori(0, more):
                        n = dve.snap(nx, min_val=0, max_val=(MAXR - 1) * E)
                        dve.wait_ge(gathered, e + (1 if last else 2))
                        V.tensor_scalar(pos[:, :, ds(e, 1)], pos[:, :, ds(e, 1)], -float(CAP), None, ALU.add).then_inc(x_clip, 1)
                        dve.wait_ge(x_clip, 2 * n + 1)
                        for a in range(TA):
                            o = S[:, a, :].rearrange("p (g s) -> p g s", g=NH)
                            V.tensor_scalar(o, iota[:, :].unsqueeze(1).broadcast_to([P, NH, CAP]),
                                            pos[:, a, ds(e, 1)], None, ALU.is_equal).then_inc(x_s, 1)
                        dve.wait_ge(x_gath, n + 1)
                        for a in range(TA):
                            o = S[:, a, :].rearrange("p (g s) -> p g s", g=NH)
                            V.tensor_scalar(o, iota[:, :].unsqueeze(1).broadcast_to([P, NH, CAP]),
                                            pos[:, a, ds(e, 1)], wts[:, a, ds(e, 1)], ALU.is_equal, ALU.mult).then_inc(x_sw, 1)
                        dve.wait_ge(x_hTd, n + 1)
                        V.tensor_copy(hTx, Xb[:, :].rearrange("p (q s) -> p q s", q=QW)).then_inc(x_hT, 1)
                        dve.wait_ge(x_gate, n + 1)
                        V.tensor_scalar(gs, G[:, :], LIMIT, None, ALU.min).then_inc(x_gmin, 1)
                        dve.wait_ge(x_sig, n + 1)
                        V.tensor_tensor(gs, gs, sg, ALU.mult).then_inc(x_gs, 1)
                        dve.wait_ge(x_up, n + 1)
                        V.tensor_scalar(ua, Ub[:, :], LIMIT, -LIMIT, ALU.min, ALU.max).then_inc(x_clip, 1)
                        dve.wait_ge(x_gs, n + 1)
                        dve.wait_ge(x_clip, 2 * n + 2)
                        V.scalar_tensor_tensor(ua, ua, 1.0, gs, ALU.add, ALU.mult).then_inc(x_act, 1)
                        dve.wait_ge(x_end, n + 1)
                        dve.reg_add(nx, nx, 1)

            with dve.Fori(0, E // 2 - 1) as i:
                for r in range(2):
                    expert(2 * i + r, r)
            expert(E - 2, 0)
            expert(E - 1, 1, last=True)

            for n in range(TA * NH):
                a, h = n // NH, n % NH
                cs = slice(h * HALF, (h + 1) * HALF)
                dve.wait_ge(y_all, 1)
                dve.wait_ge(gf_sb, min(n, NH - 1) + 1)
                step(V.tensor_tensor(HV[:, 1, cs], Yb[a][h][:, :], HV[:, 0, cs], ALU.mult))
                V.tensor_tensor(x_sb[:, a, cs], x_sb[:, a, cs], HV[:, 1, cs], ALU.add).then_inc(x3_ready, 1)
                dve.wait_ge(x3_ready, n + 1)
            for a in range(TA):
                v, s_ = stat[:, VAR3 + a:VAR3 + a + 1], SS3 + 2 * a
                dve.wait_ge(x3_sq, NH * (a + 1))
                step(V.tensor_tensor(v, stat[:, s_:s_ + 1], stat[:, s_ + 1:s_ + 2], ALU.add))
                V.tensor_scalar(v, v, 1.0 / D, EPS, ALU.mult, ALU.add).then_inc(x3_var, 1)
                dve.wait_ge(x3_std, a + 1)
                step(V.reciprocal(stat[:, RST3 + a:RST3 + a + 1], stat[:, STD3 + a:STD3 + a + 1]))
                dve.wait_ge(s_gfin, 16)
                for h in range(NH):
                    cs = slice(h * HALF, (h + 1) * HALF)
                    V.scalar_tensor_tensor(x_sb[:, a, cs], x_sb[:, a, cs], stat[:, RST3 + a:RST3 + a + 1],
                                           slot(GATE_SLOT[0])[:, cs], ALU.mult, ALU.mult).then_inc(o_ready, 1)

        @block.tensor
        def _(pe):
            M = nc.tensor.matmul
            TR = nc.tensor.transpose

            def arrived(n):
                pe.wait_ge(s_slot[n % RING], 16 * (n // RING + 1))

            pe.wait_ge(c_ident, 1)
            pe.wait_ge(s_rows, 48)
            TR(B[6][:, 0:5 * KT], rows, ident[0:5 * KT, 0:5 * KT]).then_inc(rowsT_done, 1)
            pe.wait_ge(ws_masked, 1)
            for g in range(NG):
                t = TR(B[4 + g // 4][:, P * (g % 4):P * (g % 4) + P], ws_nat[:, g, :], ident[:, :])
            t.then_inc(wsT_done, 1)
            pe.wait_ge(xn_ready, TA)
            for k in range(KT):
                for a in range(TA):
                    c = T * (k % 2) + P * a
                    t = TR(B[k // 2][:, c:c + P], HV[:, a, k * P:(k + 1) * P], ident[:, :])
            t.then_inc(xnT_done, 1)

            def modulation(i):
                if i == 0:
                    pe.wait_ge(cond_ready, 1)
                if i == 1:
                    pe.wait_ge(scale_ready, 1)
                if i == 2:
                    pe.wait_ge(mod_ready, 2)
                for q in range(4):
                    n = unit_no[("ada", i, q)]
                    arrived(n)
                    w = slot(n % RING).rearrange("p (k n) -> p k n", k=2)
                    for kk in range(2):
                        for j in range(4):
                            t = M(B[7][32 * j:32 * j + 32, :], cond[:, 2 * q + kk, :], w[:, kk, HALF * j:HALF * (j + 1)],
                                  start=(q + kk == 0), stop=(q == 3 and kk == 1))
                    t.then_inc(unit_used, 1)
                pe.wait_ge(unit_used, unit_no[("ada", i, 3)] + 1)
                pe.nop().then_inc(ada_done, 1)

            modulation(0)
            pe.wait_ge(mod_ready, 1)
            for q in range(QW):
                t = TR(B[7][:, P * q:P * q + P], mod[:, 0, P * q:P * q + P], ident[:, :])
            t.then_inc(modT_done, 1)
            pe.wait_ge(hT_dve, KT // 2)
            pe.wait_ge(hT_act, KT // 2)
            pe.wait_ge(wsT_ready, 2)
            for h in range(NH):
                n = unit_no[("in", V_, h)]
                arrived(n)
                w = slot(n % RING).rearrange("p (k n) -> p k n", k=KT)
                if h == 1:
                    pe.wait_ge(scale_ready, 1)
                for a in range(TA):
                    for k in range(KT):
                        t = M(B[4 + 2 * h + a][:, :], hT[:, k, a * P:(a + 1) * P], w[:, k, :], start=(k == 0), stop=(k == KT - 1))
                    t.then_inc(v_done, 1)
                pe.wait_ge(v_done, TA * (h + 1))
                pe.nop().then_inc(unit_used, 1)

            def spatial(c):
                if c == 0:
                    pe.wait_ge(v_ready, TA)
                    pe.wait_ge(v_gelu, TA * NH)
                else:
                    pe.wait_ge(sp_used, c)
                for g in (2 * c, 2 * c + 1):
                    for a in range(TA):
                        o = T * (g % 2) + P * a
                        t = M(B[6][:, o:o + P], HV[:, a, g * P:(g + 1) * P], wsT[:, g, :], start=True, stop=True)
                t.then_inc(sp_done, 1)

            for h in range(NH):
                for i, s in enumerate(SECTIONS):
                    n = unit_no[("in", s, h)]
                    arrived(n)
                    w = slot(n % RING).rearrange("p (k n) -> p k n", k=KT)
                    for b in range(2):
                        m = 2 * (NS * h + i) + b
                        if m >= 4 and m < 6:
                            pe.wait_ge(v_gelu, m - 3)
                        if m >= 6:
                            m0 = m - 6
                            h0, s0, b0 = m0 // (2 * NS), SECTIONS[(m0 // 2) % NS], m0 % 2
                            if s0 in (SC_X, SC_B):
                                pe.wait_ge(sec_dve, dve_bank(h0, s0, b0))
                            else:
                                pe.wait_ge(sec_act, act_bank(h0, s0, b0))
                        for tt in range(2):
                            for k in range(KT):
                                c0 = P * (2 * b + tt)
                                t = M(B[m % 6][:, T * tt:T * tt + T], w[:, k, c0:c0 + P], hT[:, k, :],
                                      start=(k == 0), stop=(k == KT - 1))
                        t.then_inc(sec_done, 1)
                        if s == U_:
                            spatial(2 * h + b)
                    pe.wait_ge(sec_done, 2 * (NS * h + i) + 2)
                    pe.nop().then_inc(unit_used, 1)
                modulation(1 + h)

            pe.wait_ge(c_late, 1)
            pe.wait_ge(mod_ready, 2)
            pe.wait_ge(sec_act, act_bank(NH - 1, GATE_B, 1))
            pe.wait_ge(sec_dve, dve_bank(NH - 1, SC_B, 1))
            pe.wait_ge(sp_used, NG // 2)
            for j in range(NH):
                M(B[4 + j][:, :], first[32 * j:32 * j + 32, :], mod[32 * j:32 * j + 32, 1, :], start=True, stop=True).then_inc(gm_done, 1)
            pe.wait_ge(m_ready, NH * NH)
            for h in range(NH):
                n = unit_no[("out", 0, h)]
                arrived(n)
                w = slot(n % RING).rearrange("p (k n) -> p k n", k=KT)
                for a in range(TA):
                    for k in range(KT):
                        t = M(B[TA * h + a][:, :], mT[:, k, a * P:(a + 1) * P], w[:, k, :], start=(k == 0), stop=(k == KT - 1))
                    t.then_inc(mix_done, 1)
                pe.wait_ge(mix_done, TA * (h + 1))
                pe.nop().then_inc(unit_used, 1)
                if h == 0:
                    pe.wait_ge(fs_row, 1)
                    for j in range(NH):
                        M(B[6 + j][:, :], first[32 * j:32 * j + 32, :], mod[32 * j:32 * j + 32, 2, :], start=True, stop=True).then_inc(fs_done, 1)
                    pe.wait_ge(gm_sb, NH)
                    for j in range(NH):
                        p0 = 32 * (2 + j)
                        M(B[4 + j][:, :], first[p0:p0 + 32, :], mod[p0:p0 + 32, 1, :], start=True, stop=True,
                          tile_position=(p0, 0)).then_inc(fh_done, 1)
            pe.wait_ge(x2_ready, TA * NH)
            for k in range(KT):
                pe.wait_ge(h2_ready, TA if k < KT // 2 else TA * NH)
                for a in range(TA):
                    c = T * (k % 2) + P * a
                    t = TR(B[k // 2][:, c:c + P], HV[:, a, k * P:(k + 1) * P], ident[:, :])
                if k % 4 == 3:
                    t.then_inc(h2T_done, 1)
            pe.wait_ge(s_rw, 32)
            pe.wait_ge(h2T_dve, 2)
            for k in range(KT):
                if k == 4:
                    pe.wait_ge(h2T_act, 2)
                j = k % 4
                t = M(B[4][32 * j:32 * j + 32, 0:T], rw[:, k, :], hT[:, k, :], start=(k < 4), stop=(k >= 4))
            t.then_inc(part_done, 1)
            pe.wait_ge(part_ready, 1)
            for a in range(TA):
                t = M(B[5][:, a * E:(a + 1) * E], part[:, a * P:(a + 1) * P], stack, start=True, stop=True)
            t.then_inc(lg_done, 1)
            pe.wait_ge(mask_ready, TA)
            M(B[6][:, 0:E], below, mask[:, 0, :], start=True, stop=True)
            M(B[6][:, E:2 * E], below, mask[:, 1, :], start=True, stop=False)
            M(B[6][:, E:2 * E], ones, mask[:, 0, :], start=False, stop=True)
            M(B[6][:, 2 * E:3 * E], ones, mask[:, 0, :], start=True, stop=False)
            M(B[6][:, 2 * E:3 * E], ones, mask[:, 1, :], start=False, stop=True).then_inc(rank_done, 1)
            pe.wait_ge(table_ready, 1)
            pe.wait_ge(s_ready, TA)

            def gather(dst, signal):
                for a in range(TA):
                    for g in range(NH):
                        t = M(dst[CAP * g:CAP * g + CAP, :], S[:, a, CAP * g:CAP * g + CAP], HV[:, a, g * HALF:(g + 1) * HALF],
                              start=(a == 0), stop=(a == TA - 1))
                t.then_inc(signal, 1)

            def turn(dst, src, signal):
                for q in range(QW):
                    t = TR(dst[:, P * q:P * q + P], src[:, P * q:P * q + P], ident[:, :])
                t.then_inc(signal, 1)

            gather(Db, gathered)
            pe.wait_ge(wts_ready, TA)
            for a in range(TA):
                t = TR(B[7][0:E, a * P:(a + 1) * P], wts[:, a, :], ident[:, :])
            t.then_inc(wT_done, 1)
            pe.wait_ge(wT_ready, 1)
            pe.wait_ge(s_bdn, 16)
            for a in range(TA):
                for g in range(NH):
                    t = M(Yb[a][g][:, :], wT[:, a * P:(a + 1) * P], b_dn[:, g * HALF:(g + 1) * HALF], start=True, stop=True)
            t.then_inc(y_open, 1)
            pe.wait_ge(hg_ready, 1)
            turn(G, hg, hTg_done)
            pe.wait_ge(swT_zero, 1)
            pe.wait_ge(s_bgu, 16)
            nx = pe.alloc_register("pe_rounds")
            pe.reg_mov(nx, 0)

            def project(dst, hsrc, r, w0, j0, sems, count):
                for g in range(NH):
                    M(dst[CAP * g:CAP * g + CAP, :], sel[r][:, j0 + g, :], b_gu[:, :], start=True, stop=False)
                for k in range(KT):
                    if k % 2 == 0 and sems is not None:
                        pe.wait_ge(sems[k // 2], count)
                    for g in range(NH):
                        t = M(dst[CAP * g:CAP * g + CAP, :], hsrc[:, k % QW, CAP * (k // QW):CAP * (k // QW) + CAP],
                              w_half(w0, k)[:, g * HALF:(g + 1) * HALF], start=False, stop=(k == KT - 1))
                return t

            def down(count):
                for k in range(KT):
                    if k % 2 == 0 and count is not None:
                        pe.wait_ge(s_down[k // 2], count)
                    for g in range(NH):
                        t = M(Db[CAP * g:CAP * g + CAP, :], actT[:, k % QW, CAP * (k // QW):CAP * (k // QW) + CAP],
                              w_half(DOWN_SLOT, k)[:, g * HALF:(g + 1) * HALF], start=(k == 0), stop=(k == KT - 1))
                return t

            def scatter(yt, st):
                for a in range(TA):
                    for g in range(NH):
                        t = M(Yb[a][g][:, :], st[CAP * g:CAP * g + CAP, a * P:(a + 1) * P], yt[CAP * g:CAP * g + CAP, :],
                              start=False, stop=True, skip_group_check=True)
                return t

            def expert(e, r, uses, last=False):
                pe.wait_ge(hTg_ready, e + 1)
                pe.wait_ge(sel_ready, e + 1)
                project(G, hTg, r, GATE_SLOT[r], 0, s_gate[r], 16 * uses).then_inc(gate_done, 1)
                pe.wait_ge(sw_ready, TA * (e + 1))
                for a in range(TA):
                    t = TR(Xb[:, a * P:(a + 1) * P], Sw[:, a, :], ident[:, :])
                t.then_inc(swT_done, 1)
                pe.wait_ge(y_ready, e + 1)
                scatter(y, SwT[1 - r])
                project(Ub, hTg, r, UP_SLOT[r], 2, s_up[r], 16 * uses).then_inc(up_done, 1)
                if not last:
                    pe.wait_ge(s_ready, TA * (e + 2))
                    gather(Db, gathered)
                pe.wait_ge(swT_ready, e + 1)
                for q in range(QW):
                    if q % 2 == 0:
                        pe.wait_ge(act_ready, 2 * e + q // 2 + 1)
                    t = TR(Xb[:, P * q:P * q + P], ua[:, P * q:P * q + P], ident[:, :])
                t.then_inc(actT_done, 1)
                if not last:
                    pe.wait_ge(hg_ready, e + 2)
                    turn(G, hg, hTg_done)
                pe.wait_ge(actT_ready, e + 1)
                down(16 * (e + 1)).then_inc(down_done, 1)
                more = pe.value_load(rounds[0:1, ds(e, 1)], min_val=0, max_val=MAXR - 1)
                with pe.If(more > 0):
                    with pe.Fori(0, more):
                        n = pe.snap(nx, min_val=0, max_val=(MAXR - 1) * E)
                        pe.wait_ge(y_ready, e + 2)
                        if not last:
                            pe.wait_ge(hTg_ready, e + 2)
                        pe.wait_ge(x_s, TA * n + TA)
                        gather(Xb, x_gath)
                        pe.wait_ge(x_hg, n + 1)
                        turn(Xb, hg, x_hTd)
                        pe.wait_ge(x_hT, n + 1)
                        project(G, hTx, r, GATE_SLOT[r], 0, None, 0).then_inc(x_gate, 1)
                        project(Ub, hTx, r, UP_SLOT[r], 2, None, 0).then_inc(x_up, 1)
                        pe.wait_ge(x_act, n + 1)
                        turn(Xb, ua, x_actTd)
                        pe.wait_ge(x_actT, n + 1)
                        pe.wait_ge(x_sw, TA * n + TA)
                        for a in range(TA):
                            t = TR(Xb[:, a * P:(a + 1) * P], S[:, a, :], ident[:, :])
                        t.then_inc(x_swTd, 1)
                        down(None).then_inc(x_down, 1)
                        pe.wait_ge(x_swT, n + 1)
                        pe.wait_ge(x_y, n + 1)
                        scatter(yx, SwTx).then_inc(x_end, 1)
                        pe.reg_add(nx, nx, 1)
                pe.wait_ge(down_done, e + 1)
                pe.nop().then_inc(passed, 1)

            with pe.Fori(0, E // 2 - 1) as i:
                for r in range(2):
                    expert(2 * i + r, r, i + 1)
            expert(E - 2, 0, E // 2)
            expert(E - 1, 1, E // 2, last=True)
            for j in range(NH):
                p0 = 32 * (2 + j)
                M(B[4 + j][:, :], kept[p0:p0 + 32, :], mod[p0:p0 + 32, 2, :], start=True, stop=True,
                  tile_position=(p0, 0)).then_inc(gf_done, 1)
            pe.wait_ge(y_ready, E + 1)
            pe.wait_ge(swT_ready, E)
            scatter(y, SwT[1]).then_inc(y_all, 1)


_INS = ["x", "c", "w_ada", "b_ada", "norm_mix_g", "w_in", "conv_w", "w_spatial", "b_spatial", "ln_v_g",
        "w_out", "norm_ffn_g", "router_w", "router_b", "w_gate_up", "b_gate_up", "w_down", "b_down",
        "final_norm_g"]


def kernel(**inputs):
    import numpy as _np
    import concourse.bacc as _bacc
    from concourse import mybir as _mybir
    from concourse.bass_utils import run_bass_kernel_spmd as _run

    nc = _bacc.Bacc("TRN2", target_bir_lowering=False, num_devices=1)
    arrays, args = {}, []
    for name in _INS:
        a = _np.ascontiguousarray(inputs[name])
        arrays[f"in_{name}_dram"] = a
        args.append(nc.dram_tensor(f"in_{name}_dram", a.shape, _mybir.dt.from_np(a.dtype), kind="ExternalInput").ap())
    shape = tuple(inputs["x"].shape)
    args.append(nc.dram_tensor("out_0_dram", shape, _mybir.dt.float32, kind="ExternalOutput").ap())
    hybrid_trunk(nc, *args)
    r = _run(nc, [arrays], core_ids=[0])
    return r.results[0]["out_0_dram"]
```

```python
import concourse.bass as bass
from concourse import mybir
from contextlib import ExitStack


def hybrid_trunk(nc, x_in, c_in, w_ada, b_ada, norm_mix_g, w_in, conv_w, w_spatial, b_spatial, ln_v_g,
                 w_out, norm_ffn_g, router_w, router_b, w_gate_up, b_gate_up, w_down, b_down,
                 final_norm_g, out):
    f32, i32, u32, bf16 = mybir.dt.float32, mybir.dt.int32, mybir.dt.uint32, mybir.dt.bfloat16
    ALU, ACT, AX = mybir.AluOpType, mybir.ActivationFunctionType, mybir.AxisListType
    ds = bass.ds

    P = 128
    DEPTH, D, D_IN = w_in.shape
    T = x_in.shape[1]
    E = router_w.shape[2]
    FF = w_down.shape[2]
    NG = w_spatial.shape[1]
    TOP_K = 4
    LIMIT, ALPHA, EPS = 7.0, 1.702, 1e-6
    TA = T // P
    KT = D // P
    HALF = 512
    NH = D // HALF
    CAP = 32
    MAXR = T // CAP
    NQ = P // CAP
    QC = D // NQ
    KQ = QC // P
    ALL_ROUNDS = T * TOP_K // CAP + E
    PARTS = 3
    QW = HALF // P
    assert DEPTH == 1 and T == 2 * P and D == 2 * HALF and FF == D and NG == KT and E == 32

    SC_X, SC_B, SC_C, U_, V_, GATE_A, GATE_B = range(7)
    SECTIONS = [SC_C, SC_X, SC_B, GATE_A, U_, GATE_B]
    NS = len(SECTIONS)

    UW = KT * HALF
    RING = 8
    SLOTS = 10
    units = [("ada", 0, q) for q in range(4)] + [("in", V_, h) for h in range(NH)]
    for h in range(NH):
        units += [("in", s, h) for s in SECTIONS]
        units += [("ada", 1 + h, q) for q in range(4)]
    units += [("out", 0, h) for h in range(NH)]
    unit_no = {u: n for n, u in enumerate(units)}
    NU = len(units)

    ctx = ExitStack()
    with ctx:
        def sb(name, shape, dt=f32):
            return ctx.enter_context(nc.sbuf_tensor(name, shape, dt))

        def sem(name):
            return ctx.enter_context(nc.semaphore(name))

        W = sb("W", [P, SLOTS * UW])
        x_sb = sb("x_sb", [P, TA, D])
        HV = sb("HV", [P, TA, D])
        hT = sb("hT", [P, KT, T])
        mT = sb("mT", [P, KT, T])
        mod = sb("mod", [P, 3, HALF])
        EW = sb("EW", [P, 3 * HALF])
        b_gu = sb("b_gu", [P, HALF])
        ident = sb("ident", [P, P])
        iota = sb("iota", [P, CAP])
        pos = sb("pos", [P, TA, E])
        wts = sb("wts", [P, TA, E])
        cols = sb("cols", [P, 5 * KT])
        stat = sb("stat", [P, 64])
        rounds = sb("rounds", [1, E], i32)

        def slot(n, k=1):
            return W[:, n * UW:(n + k) * UW]

        tmp = W[:, RING * UW:SLOTS * UW]
        accA = tmp[:, 0:D].rearrange("p (t n) -> p t n", n=T)
        accB = tmp[:, D:2 * D].rearrange("p (t n) -> p t n", n=T)
        accC = tmp[:, 2 * D:3 * D].rearrange("p (t n) -> p t n", n=T)
        ws_nat = tmp[:, 0:D].rearrange("p (g s) -> p g s", g=NG)
        bs_all = tmp[:, 3 * D:4 * D].rearrange("p (g t) -> p g t", g=NG)
        wsT = tmp[:, 4 * D:5 * D].rearrange("p (g t) -> p g t", g=NG)
        lng = tmp[:, 5 * D:6 * D]
        late = tmp[:, 6 * D:8 * D]
        below = late[:, 0:P]
        ones = late[:, P:2 * P]
        rw = late[:, 3 * P:3 * P + KT * E].rearrange("p (k e) -> p k e", k=KT)
        cond = late[:, 5 * P:5 * P + KT * 32].rearrange("p (k r) -> p k r", k=KT)
        stack = late[:, 7 * P:7 * P + E]
        rb = late[:, 7 * P + E:7 * P + 2 * E]
        cT = late[:, 7 * P + 2 * E:7 * P + 2 * E + KT]
        shm = late[:, 7 * P + 2 * E + KT:7 * P + 2 * E + 2 * KT]
        scm = late[:, 7 * P + 2 * E + 2 * KT:7 * P + 2 * E + 3 * KT]
        sig = late[:, 8 * P:8 * P + HALF]
        stmp = late[:, 8 * P + HALF:8 * P + 2 * HALF]
        junk = [tmp[:, D:2 * D], tmp[:, 2 * D:3 * D]]
        rows = EW[0:5 * KT, HALF:HALF + P]
        gffn = EW[0:64, 2 * HALF:3 * HALF]
        b_dn = EW[:, 0:2 * HALF]
        part = EW[:, 2 * HALF:2 * HALF + T]
        wT = EW[:, 2 * HALF + T:2 * HALF + 2 * T]
        onehot = mod[:, 0, 0:8 * E].rearrange("p (n e) -> p n e", e=E)
        logits = mod[:, 0, 8 * E:10 * E].rearrange("p (a e) -> p a e", a=TA)
        mask = mod[:, 0, 10 * E:12 * E].rearrange("p (a e) -> p a e", a=TA)
        top = mod[:, 0, 12 * E:12 * E + 16].rearrange("p (a j) -> p a j", a=TA)
        topi = mod[:, 0, 12 * E + 16:12 * E + 32].bitcast(u32).rearrange("p (a j) -> p a j", a=TA)
        topf = mod[:, 0, 12 * E + 32:12 * E + 48].rearrange("p (a j) -> p a j", a=TA)
        topw = mod[:, 0, 12 * E + 48:12 * E + 56].rearrange("p (a j) -> p a j", a=TA)
        negm = mod[:, 0, 12 * E + 56:12 * E + 58]
        esum = mod[:, 0, 12 * E + 58:12 * E + 60]
        over = mod[0:1, 0, 0:E * (MAXR - 1)].rearrange("p (e m) -> p e m", e=E)
        nover = mod[0:1, 0, E * (MAXR - 1):E * MAXR]

        def w_half(n, rows_):
            return slot(n, 2).rearrange("p (k n) -> p k n", k=KT)[:, rows_, :]

        PAIRS = SLOTS // 2
        GATE, UP, DOWN = range(3)
        TURN = PAIRS
        TURNS = (E - 2) // TURN
        assert TURNS * TURN + 2 == E

        def block_slot(b):
            return 2 * ((b + 2) % PAIRS)

        def block_uses(b):
            return b // PAIRS + 1

        work = mT[:, :, :].rearrange("p k t -> p (k t)")
        S = work[:, 0:256].rearrange("p (a s) -> p a s", a=TA)
        Sw = work[:, 256:512].rearrange("p (a s) -> p a s", a=TA)
        SwT = work[:, 512:512 + T]
        hg = work[:, 768:768 + QC]
        hTg = work[:, 1024:1024 + QC].rearrange("p (q s) -> p q s", q=KQ)
        actT = work[:, 1280:1280 + QC].rearrange("p (q s) -> p q s", q=KQ)
        wts4 = work[:, 1280:1280 + TA * P].rearrange("p (a n) -> p a n", a=TA)
        sel = work[:, 1536:1536 + P].rearrange("p (j s) -> p j s", j=4)
        work2 = hT[:, :, :].rearrange("p k t -> p (k t)")
        yw = work2[:, 0:QC]
        yr = work2[:, QC:2 * QC]
        yp = work2[:, 2 * QC:2 * QC + PARTS * QC // 2].bitcast(bf16).rearrange("p (m n) -> p m n", m=PARTS)
        ST = work2[:, 4 * QC:4 * QC + T // 2].bitcast(bf16)
        gs, sg, ua = EW[:, 0:QC], EW[:, HALF:HALF + QC], EW[:, 2 * HALF:2 * HALF + QC]

        gfin = slot(block_slot(3 * (E - 2) + UP))[:, 0:D]

        B = [ctx.enter_context(nc.psum_tensor(f"B{n}", [P, HALF], f32)) for n in range(8)]
        Yb = B[0:NQ]
        G, Ub, Db, Xb = B[4], B[5], B[6], B[7]

        s_x = sem("s_x"); s_rows = sem("s_rows"); s_bada = sem("s_bada"); s_gffn = sem("s_gffn")
        s_ws = sem("s_ws"); s_bs = sem("s_bs"); s_lng = sem("s_lng"); s_rw = sem("s_rw")
        s_bgu = sem("s_bgu"); s_bdn = sem("s_bdn"); s_gfin = sem("s_gfin"); s_out = sem("s_out")
        s_slot = [sem(f"s_slot{n}") for n in range(RING)]
        unit_used = sem("unit_used")
        c_ident = sem("c_ident"); c_iota = sem("c_iota"); c_late = sem("c_late"); pool_step = sem("pool_step")
        ws_masked = sem("ws_masked")
        dve_step = sem("dve_step")
        act_step = sem("act_step")
        x_sq = sem("x_sq"); x_var = sem("x_var"); x_std = sem("x_std"); xn_ready = sem("xn_ready")
        xnT_done = sem("xnT_done"); rowsT_done = sem("rowsT_done"); cols_ready = sem("cols_ready")
        silu_done = sem("silu_done"); cond_ready = sem("cond_ready")
        ada_done = sem("ada_done"); mod_ready = sem("mod_ready"); modT_done = sem("modT_done")
        scale_ready = sem("scale_ready"); hT_act = sem("hT_act"); hT_dve = sem("hT_dve")
        wsT_done = sem("wsT_done"); wsT_ready = sem("wsT_ready")
        v_done = sem("v_done"); v_gelu = sem("v_gelu"); v_mu = sem("v_mu"); v_sq = sem("v_sq")
        v_var = sem("v_var"); v_std = sem("v_std"); v_ready = sem("v_ready")
        sec_done = sem("sec_done")
        sec_act = sem("sec_act")
        sec_dve = sem("sec_dve")
        sp_done = sem("sp_done"); sp_used = sem("sp_used"); m_ready = sem("m_ready")
        mix_done = sem("mix_done"); gm_done = sem("gm_done"); gm_sb = sem("gm_sb")
        x2_ready = sem("x2_ready"); x2_sq = sem("x2_sq"); x2_var = sem("x2_var"); x2_std = sem("x2_std")
        fs_row = sem("fs_row"); fs_done = sem("fs_done"); fh_done = sem("fh_done")
        h2_ready = sem("h2_ready"); h2T_done = sem("h2T_done"); h2T_act = sem("h2T_act"); h2T_dve = sem("h2T_dve")
        part_done = sem("part_done"); part_ready = sem("part_ready"); lg_done = sem("lg_done")
        top_ready = sem("top_ready"); exp_done = sem("exp_done"); mask_ready = sem("mask_ready")
        wts_ready = sem("wts_ready"); rank_done = sem("rank_done"); wT_done = sem("wT_done")
        wT_ready = sem("wT_ready"); table_ready = sem("table_ready"); y_zero = sem("y_zero"); pos_moved = sem("pos_moved"); over_ready = sem("over_ready")
        y_open = sem("y_open"); dn_zero = sem("dn_zero"); yw_ready = sem("yw_ready"); st_ready = sem("st_ready"); y_cut = sem("y_cut"); y_rest = sem("y_rest")
        s_block = [[sem(f"s_block{r}{q}") for q in range(4)] for r in range(PAIRS)]
        s_ready = sem("s_ready"); sw_ready = sem("sw_ready"); sel_ready = sem("sel_ready")
        gathered = sem("gathered"); hg_ready = sem("hg_ready"); hTg_done = sem("hTg_done")
        hTg_ready = sem("hTg_ready"); gate_done = sem("gate_done"); gmin_ready = sem("gmin_ready")
        sig_ready = sem("sig_ready"); gs_ready = sem("gs_ready"); swT_done = sem("swT_done")
        swT_ready = sem("swT_ready"); up_done = sem("up_done"); clip_done = sem("clip_done")
        act_ready = sem("act_ready"); actT_done = sem("actT_done"); actT_ready = sem("actT_ready")
        down_done = sem("down_done"); y_ready = sem("y_ready"); released = sem("released")
        y_all = sem("y_all"); gf_done = sem("gf_done"); gf_sb = sem("gf_sb"); x3_ready = sem("x3_ready")
        x3_sq = sem("x3_sq"); x3_var = sem("x3_var"); x3_std = sem("x3_std"); o_ready = sem("o_ready")

        ada_v = w_ada[0].rearrange("(q k p) n -> q p k n", k=2, p=P)
        in_v = w_in[0].rearrange("(k p) n -> p k n", p=P)
        out_v = w_out[0].rearrange("(k p) n -> p k n", p=P)
        gu_v = w_gate_up[0].rearrange("e (q k p) n -> e q p k n", k=2, p=P)
        dn_v = w_down[0].rearrange("e (q k p) n -> e q p k n", k=2, p=P)

        SS, VAR, STD, RST = 0, 4, 6, 8
        VS, NMU, VSS, VVAR, VSTD, VRST = 10, 14, 16, 18, 20, 22
        SS2, VAR2, STD2, RST2 = 24, 30, 32, 34
        SS3, VAR3, STD3, RST3 = 36, 42, 44, 46
        WSL = 48

        dve_order = [(h, s, b) for h in range(NH) for s in SECTIONS if s not in (SC_C, U_) for b in range(2)]

        def dve_bank(h, s, b):
            return dve_order.index((h, s, b)) + 1

        act_order = [(h, s, b) for h in range(NH) for s in SECTIONS if s in (SC_C, GATE_A, U_, GATE_B) for b in range(2)]

        def act_bank(h, s, b):
            return act_order.index((h, s, b)) + 1

        block = ctx.enter_context(nc.Block())

        @block.sync
        def _(sp):
            sp.dma_start(rows[4 * KT:5 * KT, :], c_in[0].rearrange("(k p) -> k p", p=P)).then_inc(s_rows, 16)
            sp.dma_start(rows[0:KT, :], norm_mix_g[0].rearrange("(k p) -> k p", p=P)).then_inc(s_rows, 16)
            sp.dma_start(rows[KT:4 * KT, :], conv_w[0].rearrange("j (k p) -> (j k) p", p=P)).then_inc(s_rows, 16)
            sp.dma_start(x_sb[:, :, :], x_in[0].rearrange("(a p) n -> p a n", p=P)).then_inc(s_x, 16)
            for n, (kind, s, h) in enumerate(units):
                if n >= RING:
                    sp.wait_ge(unit_used, n - RING + 1)
                if kind == "ada":
                    src = ada_v[h, :, :, 4 * HALF * s:4 * HALF * (s + 1)]
                    dst = slot(n % RING).rearrange("p (k n) -> p k n", k=2)
                else:
                    c0 = (s * D if kind == "in" else 0) + h * HALF
                    src = (in_v if kind == "in" else out_v)[:, :, c0:c0 + HALF]
                    dst = slot(n % RING).rearrange("p (k n) -> p k n", k=KT)
                sp.dma_start(dst, src).then_inc(s_slot[n % RING], 16)

            def load(b, e, qs=range(4)):
                src = (gu_v[e, :, :, :, 0:FF], gu_v[e, :, :, :, FF:2 * FF], dn_v[e, :, :, :, :])[b % 3]
                for q in qs:
                    sp.dma_start(w_half(block_slot(b), slice(2 * q, 2 * q + 2)), src[q]).then_inc(s_block[b % PAIRS][q], 16)

            sp.wait_ge(unit_used, NU - RING + 4)
            load(0, 0)
            load(1, 0)
            sp.wait_ge(m_ready, NH * NH)
            load(2, 0, (0, 1, 2))
            sp.wait_ge(unit_used, NU)
            load(3, 1)
            load(4, 1)
            sp.wait_ge(table_ready, 1)
            load(2, 0, (3,))
            with sp.Fori(0, TURNS) as i:
                for b in range(PAIRS, PAIRS + 3 * TURN):
                    sp.wait_ge(released, 3 * TURN * i + b - PAIRS + 1)
                    load(b, TURN * i + b // 3)
            b = 3 * E - 1
            sp.wait_ge(released, b - PAIRS + 1)
            load(b, E - 1)
            sp.wait_ge(released, 3 * (E - 2) + UP + 1)
            sp.dma_start(gfin, final_norm_g[:].partition_broadcast(P)).then_inc(s_gfin, 16)
            for a in range(TA):
                sp.wait_ge(o_ready, NH * (a + 1))
                sp.dma_start(out[0, a * P:(a + 1) * P, :], x_sb[:, a, :]).then_inc(s_out, 16)
            sp.wait_ge(s_out, 16 * TA)

        @block.gpsimd
        def _(pool):
            done = [0]

            def one(ins, signal):
                ins.then_inc(pool_step, 1)
                done[0] += 1
                pool.wait_ge(pool_step, done[0])
                if signal is not None:
                    pool.nop().then_inc(signal, 1)

            G_ = nc.gpsimd
            one(G_.memset(ident[:, :], 0.0), None)
            one(G_.affine_select(out=ident[:, :], in_=ident[:, :], compare_op=ALU.not_equal, fill=1.0,
                                 base=0, pattern=[[-1, P]], channel_multiplier=1), c_ident)
            one(G_.iota(iota[:, :], pattern=[[1, CAP]], base=0, channel_multiplier=0,
                        allow_small_or_imprecise_dtypes=True), c_iota)
            pool.wait_ge(s_ws, 16)
            one(G_.affine_select(out=ws_nat, in_=ws_nat, compare_op=ALU.is_ge, fill=0.0,
                                 base=0, pattern=[[0, NG], [-1, P]], channel_multiplier=1), ws_masked)
            pool.wait_ge(cols_ready, 1)
            one(G_.memset(b_dn[E:2 * E, :], 0.0), None)
            one(G_.memset(b_dn[2 * E:4 * E, :], 0.0), dn_zero)
            one(G_.memset(below, 1.0), None)
            one(G_.affine_select(out=below, in_=below, compare_op=ALU.is_gt, fill=0.0,
                                 base=0, pattern=[[1, P]], channel_multiplier=-1), None)
            one(G_.memset(ones, 1.0), None)
            one(G_.memset(stack, 0.0), None)
            for j in range(4):
                v = stack[32 * j:32 * j + 32, :]
                one(G_.affine_select(out=v, in_=v, compare_op=ALU.not_equal, fill=1.0,
                                     base=0, pattern=[[-1, E]], channel_multiplier=1), c_late if j == 3 else None)
            pool.wait_ge(lg_done, 1)
            one(G_.memset(yp, 0.0), y_zero)
            one(G_.memset(ST, 0.0), y_zero)
            pool.nop().then_inc(yw_ready, 1)
            pool.nop().then_inc(y_ready, 1)
            pool.nop().then_inc(swT_ready, 1)
            pool.nop().then_inc(st_ready, 1)

        @block.scalar
        def _(act):
            A = nc.scalar.activation
            ba = b_ada[0].rearrange("(i j n) -> j i n", i=3, j=4)
            for j in range(4):
                act.dma_start(mod[32 * j:32 * j + 32, :, :], ba[j].partition_broadcast(32)).then_inc(s_bada, 16)
            act.dma_start(ws_nat, w_spatial[0].rearrange("g t s -> t g s")).then_inc(s_ws, 16)
            act.dma_start(bs_all, b_spatial[0].partition_broadcast(P)).then_inc(s_bs, 16)
            act.dma_start(lng, ln_v_g[0].partition_broadcast(P)).then_inc(s_lng, 16)
            gf = norm_ffn_g[0].rearrange("(j n) -> j n", j=NH)
            for j in range(NH):
                act.dma_start(gffn[32 * j:32 * j + 32, :], gf[j].partition_broadcast(32)).then_inc(s_gffn, 16)
            act.dma_start(rw, router_w[0].rearrange("(k p) e -> p k e", p=P)).then_inc(s_rw, 16)
            act.dma_start(rb, router_b[0].partition_broadcast(P)).then_inc(s_rw, 16)
            act.dma_start(b_gu[:, :], b_gate_up[0].rearrange("e (j n) -> (e j) n", j=4)).then_inc(s_bgu, 16)

            act.wait_ge(s_x, 16)
            for a in range(TA):
                A(junk[a], x_sb[:, a, :], ACT.Square, accum_out=stat[:, SS + a:SS + a + 1]).then_inc(x_sq, 1)
            act.wait_ge(x_var, 1)
            A(stat[:, STD:STD + TA], stat[:, VAR:VAR + TA], ACT.Sqrt).then_inc(x_std, 1)
            act.wait_ge(cols_ready, 1)
            A(cT, cols[:, 4 * KT:5 * KT], ACT.Silu).then_inc(silu_done, 1)
            act.dma_start(b_dn[0:E, :], b_down[0]).then_inc(s_bdn, 16)
            act.wait_ge(xnT_done, 1)
            act.wait_ge(scale_ready, 1)
            for k in range(KT // 2, KT):
                A(hT[:, k, :], B[k // 2][:, T * (k % 2):T * (k % 2) + T], ACT.Identity,
                  scale=scm[:, k:k + 1], bias=shm[:, k:k + 1]).then_inc(hT_act, 1)
            for h in range(NH):
                for a in range(TA):
                    act.wait_ge(v_done, NH * h + a + 1)
                    A(HV[:, a, h * HALF:(h + 1) * HALF], B[4 + 2 * h + a][:, :], ACT.Gelu,
                      accum_out=stat[:, VS + 2 * a + h:VS + 2 * a + h + 1]).then_inc(v_gelu, 1)
            act.wait_ge(v_mu, 1)
            for a in range(TA):
                A(junk[a], HV[:, a, :], ACT.Square, bias=stat[:, NMU + a:NMU + a + 1],
                  accum_out=stat[:, VSS + a:VSS + a + 1]).then_inc(v_sq, 1)
            act.wait_ge(v_var, 1)
            A(stat[:, VSTD:VSTD + TA], stat[:, VVAR:VVAR + TA], ACT.Sqrt).then_inc(v_std, 1)
            for h in range(NH):
                for n, s in enumerate(SECTIONS):
                    for b in range(2):
                        m = 2 * (NS * h + n) + b
                        bank = B[m % 6][:, :]
                        if s in (SC_X, SC_B):
                            continue
                        act.wait_ge(sec_done, m + 1)
                        if s == SC_C:
                            if h == 0 and b == 0:
                                act.wait_ge(wsT_done, 1)
                            if h > 0:
                                act.wait_ge(m_ready, NH * (h - 1) + b + 1)
                            A(accA[:, 2 * b:2 * b + 2, :], bank.rearrange("p (t n) -> p t n", n=T), ACT.Copy).then_inc(sec_act, 1)
                        elif s == U_:
                            if h > 0:
                                act.wait_ge(m_ready, NH * (h - 1) + b + 1)
                            A(accC[:, 2 * b:2 * b + 2, :], bank.rearrange("p (t n) -> p t n", n=T), ACT.Gelu).then_inc(sec_act, 1)
                        else:
                            if s == GATE_A and b == 0 and h > 0:
                                act.wait_ge(sec_dve, dve_bank(h - 1, GATE_B, 1))
                            if s == GATE_A and b == 1:
                                act.wait_ge(sec_dve, dve_bank(h, GATE_A, 0))
                            if s == GATE_B:
                                act.wait_ge(sec_dve, dve_bank(h, GATE_A, 1) if b == 0 else dve_bank(h, GATE_B, 0))
                            A(sig, bank, ACT.Sigmoid).then_inc(sec_act, 1)
            for h in range(NH):
                act.wait_ge(gm_done, h + 1)
                A(HV[:, 0, h * HALF:(h + 1) * HALF], B[4 + h][:, :], ACT.Copy).then_inc(gm_sb, 1)
            for n in range(TA * NH):
                act.wait_ge(x2_ready, n + 1)
                a, h = n % TA, n // TA
                A(sig if n % 2 else stmp, x_sb[:, a, h * HALF:(h + 1) * HALF], ACT.Square,
                  accum_out=stat[:, SS2 + 2 * a + h:SS2 + 2 * a + h + 1]).then_inc(x2_sq, 1)
                act.wait_ge(x2_sq, n + 1)
            act.wait_ge(x2_var, 1)
            A(stat[:, STD2:STD2 + TA], stat[:, VAR2:VAR2 + TA], ACT.Sqrt).then_inc(x2_std, 1)
            act.wait_ge(h2T_done, 2)
            for b in (2, 3):
                A(hT[:, 2 * b:2 * b + 2, :], B[b][:, :].rearrange("p (k t) -> p k t", t=T), ACT.Copy).then_inc(h2T_act, 1)
            act.wait_ge(top_ready, 1)
            for a in range(TA):
                A(topw[:, a, :], top[:, a, 0:TOP_K], ACT.Exp, bias=negm[:, a:a + 1],
                  accum_out=esum[:, a:a + 1]).then_inc(exp_done, 1)
            act.wait_ge(wT_done, 1)
            A(wT, B[7][:, 0:T], ACT.Copy).then_inc(wT_ready, 1)

            act.wait_ge(gathered, 1)
            A(hg, Db[:, 0:QC], ACT.Copy).then_inc(hg_ready, 1)
            rnd = act.alloc_register("act_round")
            act.reg_mov(rnd, 0)

            def one_round(last=False):
                n = act.snap(rnd, min_val=0, max_val=ALL_ROUNDS)
                act.wait_ge(gmin_ready, n + 1)
                A(sg, gs, ACT.Sigmoid, scale=ALPHA).then_inc(sig_ready, 1)
                if not last:
                    act.wait_ge(gathered, n + 2)
                    A(hg, Db[:, 0:QC], ACT.Copy).then_inc(hg_ready, 1)
                act.wait_ge(actT_done, n + 1)
                A(actT, Xb[:, 0:QC].rearrange("p (q s) -> p q s", q=KQ), ACT.Copy).then_inc(actT_ready, 1)
                act.wait_ge(swT_done, n + 1)
                A(SwT, Ub[:, 0:T], ACT.Copy, accum_out=stat[:, WSL:WSL + 1]).then_inc(swT_ready, 1)
                act.wait_ge(down_done, n + 1)
                act.wait_ge(swT_ready, n + 2)
                A(yw, Db[:, 0:QC], ACT.Copy, scale=stat[:, WSL:WSL + 1]).then_inc(yw_ready, 1)
                act.reg_add(rnd, rnd, 1)

            def expert(e, last=False):
                more = act.value_load(rounds[0:1, ds(e, 1)], min_val=0, max_val=MAXR - 1)
                with act.If(more > 0):
                    with act.Fori(0, more):
                        one_round()
                one_round(last)

            act.wait_ge(table_ready, 1)
            with act.Fori(0, TURNS) as i:
                for r in range(TURN):
                    expert(TURN * i + r)
            expert(E - 2)
            expert(E - 1, last=True)

            for h in range(NH):
                act.wait_ge(gf_done, h + 1)
                A(HV[:, 0, h * HALF:(h + 1) * HALF], B[4 + h][:, :], ACT.Copy).then_inc(gf_sb, 1)
            for n in range(TA * NH):
                act.wait_ge(x3_ready, n + 1)
                a, h = n // NH, n % NH
                A(EW[:, HALF * (n % 2):HALF * (n % 2) + HALF], x_sb[:, a, h * HALF:(h + 1) * HALF], ACT.Square,
                  accum_out=stat[:, SS3 + 2 * a + h:SS3 + 2 * a + h + 1]).then_inc(x3_sq, 1)
                act.wait_ge(x3_sq, n + 1)
                if n % NH == NH - 1:
                    act.wait_ge(x3_var, a + 1)
                    A(stat[:, STD3 + a:STD3 + a + 1], stat[:, VAR3 + a:VAR3 + a + 1], ACT.Sqrt).then_inc(x3_std, 1)

        @block.vector
        def _(dve):
            V = nc.vector
            steps = [0]

            def step(ins):
                steps[0] += 1
                ins.then_inc(dve_step, 1)
                dve.wait_ge(dve_step, steps[0])

            dve.wait_ge(x_sq, TA)
            V.tensor_scalar(stat[:, VAR:VAR + TA], stat[:, SS:SS + TA], 1.0 / D, EPS, ALU.mult, ALU.add).then_inc(x_var, 1)
            dve.wait_ge(x_std, 1)
            step(V.reciprocal(stat[:, RST:RST + TA], stat[:, STD:STD + TA]))
            for a in range(TA):
                V.tensor_scalar(HV[:, a, :], x_sb[:, a, :], stat[:, RST + a:RST + a + 1], None, ALU.mult).then_inc(xn_ready, 1)
            dve.wait_ge(rowsT_done, 1)
            V.tensor_copy(cols[:, :], B[6][:, 0:5 * KT]).then_inc(cols_ready, 1)
            dve.wait_ge(silu_done, 1)
            V.tensor_copy(cond, cT.unsqueeze(2).broadcast_to([P, KT, 32])).then_inc(cond_ready, 1)
            def add_bias(i):
                if i == 0:
                    dve.wait_ge(s_bada, 64)
                dve.wait_ge(ada_done, i + 1)
                V.tensor_tensor(mod[:, i, :], B[7][:, :], mod[:, i, :], ALU.add).then_inc(mod_ready, 1)

            add_bias(0)
            dve.wait_ge(modT_done, 1)
            mt = B[7][:, :].rearrange("p (q j r) -> p j q r", q=QW, j=4)
            step(V.tensor_copy(shm.rearrange("p (j q) -> p j q", j=NH), mt[:, 0:2, :, 0]))
            dve.wait_ge(cols_ready, 1)
            V.scalar_tensor_tensor(scm.rearrange("p (j q) -> p j q", j=NH), mt[:, 2:4, :, 0], 1.0,
                                   cols[:, 0:KT].rearrange("p (j q) -> p j q", j=NH), ALU.add, ALU.mult).then_inc(scale_ready, 1)
            dve.wait_ge(scale_ready, 1)
            dve.wait_ge(xnT_done, 1)
            for k in range(KT // 2):
                V.tensor_scalar(hT[:, k, :], B[k // 2][:, T * (k % 2):T * (k % 2) + T],
                                scm[:, k:k + 1], shm[:, k:k + 1], ALU.mult, ALU.add).then_inc(hT_dve, 1)
            dve.wait_ge(wsT_done, 1)
            for b in range(2):
                V.tensor_copy(wsT[:, 4 * b:4 * b + 4, :], B[2 + b][:, :].rearrange("p (g t) -> p g t", t=P)).then_inc(wsT_ready, 1)
            dve.wait_ge(v_gelu, TA * NH)
            step(V.tensor_tensor(stat[:, NMU:NMU + TA], stat[:, VS:VS + 4:2], stat[:, VS + 1:VS + 4:2], ALU.add))
            V.tensor_scalar(stat[:, NMU:NMU + TA], stat[:, NMU:NMU + TA], -1.0 / D, None, ALU.mult).then_inc(v_mu, 1)
            dve.wait_ge(v_sq, TA)
            V.tensor_scalar(stat[:, VVAR:VVAR + TA], stat[:, VSS:VSS + TA], 1.0 / D, EPS, ALU.mult, ALU.add).then_inc(v_var, 1)
            dve.wait_ge(v_std, 1)
            step(V.reciprocal(stat[:, VRST:VRST + TA], stat[:, VSTD:VSTD + TA]))
            dve.wait_ge(s_lng, 16)
            for a in range(TA):
                step(V.tensor_scalar(HV[:, a, :], HV[:, a, :], stat[:, NMU + a:NMU + a + 1],
                                     stat[:, VRST + a:VRST + a + 1], ALU.add, ALU.mult))
                V.tensor_tensor(HV[:, a, :], HV[:, a, :], lng, ALU.mult).then_inc(v_ready, 1)

            def tiles(bank):
                return bank[:, :].rearrange("p (t n) -> p t n", n=T)

            dve.wait_ge(s_bs, 16)
            for h in range(NH):
                for n, s in enumerate(SECTIONS):
                    for b in range(2):
                        m = 2 * (NS * h + n) + b
                        bank = tiles(B[m % 6])
                        two = slice(2 * b, 2 * b + 2)
                        if s == SC_X:
                            dve.wait_ge(sec_done, m + 1)
                            dve.wait_ge(sec_act, act_bank(h, SC_C, b))
                            if h > 0:
                                dve.wait_ge(m_ready, NH * h)
                            V.tensor_tensor(accA[:, two, :], accA[:, two, :], bank, ALU.mult).then_inc(sec_dve, 1)
                            dve.wait_ge(sec_dve, dve_bank(h, s, b))
                            for t in (2 * b, 2 * b + 1):
                                k = 4 * h + t
                                w = [cols[:, KT * (1 + j) + k:KT * (1 + j) + k + 1] for j in range(3)]
                                step(V.tensor_scalar(accB[:, t, :], accA[:, t, :], w[2], None, ALU.mult))
                                step(V.scalar_tensor_tensor(accB[:, t, 1:T], accA[:, t, 0:T - 1], w[1], accB[:, t, 1:T], ALU.mult, ALU.add))
                                step(V.scalar_tensor_tensor(accB[:, t, 2:T], accA[:, t, 0:T - 2], w[0], accB[:, t, 2:T], ALU.mult, ALU.add))
                        elif s == SC_B:
                            dve.wait_ge(sec_done, m + 1)
                            V.tensor_tensor(accB[:, two, :], accB[:, two, :], bank, ALU.mult).then_inc(sec_dve, 1)
                            dve.wait_ge(sec_dve, dve_bank(h, s, b))
                        elif s == GATE_A:
                            dve.wait_ge(sec_act, act_bank(h, s, b))
                            V.tensor_tensor(accB[:, two, :], accB[:, two, :], tiles(sig), ALU.mult).then_inc(sec_dve, 1)
                        elif s == U_:
                            c = 2 * h + b
                            dve.wait_ge(sp_done, c + 1)
                            bias = bs_all[:, 4 * h + 2 * b:4 * h + 2 * b + 2, :].unsqueeze(2).broadcast_to([P, 2, TA, P])
                            V.tensor_tensor(stmp.rearrange("p (t a n) -> p t a n", t=2, a=TA),
                                            B[6][:, :].rearrange("p (t a n) -> p t a n", t=2, a=TA), bias, ALU.add).then_inc(sp_used, 1)
                            dve.wait_ge(sp_used, c + 1)
                            dve.wait_ge(sec_act, act_bank(h, s, b))
                            step(V.tensor_tensor(accC[:, two, :], accC[:, two, :], tiles(stmp), ALU.mult))
                        elif s == GATE_B:
                            dve.wait_ge(sec_act, act_bank(h, s, b))
                            V.tensor_tensor(accC[:, two, :], accC[:, two, :], tiles(sig), ALU.mult).then_inc(sec_dve, 1)
                            dve.wait_ge(sec_dve, dve_bank(h, s, b))
                            V.tensor_tensor(mT[:, 4 * h + 2 * b:4 * h + 2 * b + 2, :], accB[:, two, :], accC[:, two, :], ALU.add).then_inc(m_ready, 1)
                if h == 0:
                    add_bias(1)
            add_bias(2)
            dve.wait_ge(s_gffn, 16 * NH)
            dve.wait_ge(mod_ready, 3)
            V.scalar_tensor_tensor(mod[0:64, 2, :], mod[0:64, 2, :], 1.0, gffn, ALU.add, ALU.mult).then_inc(fs_row, 1)
            for n in range(TA * NH):
                a, h = n % TA, n // TA
                cs = slice(h * HALF, (h + 1) * HALF)
                dve.wait_ge(mix_done, n + 1)
                dve.wait_ge(gm_sb, h + 1)
                step(V.tensor_tensor(HV[:, 1, cs], B[n][:, :], HV[:, 0, cs], ALU.mult))
                V.tensor_tensor(x_sb[:, a, cs], x_sb[:, a, cs], HV[:, 1, cs], ALU.add).then_inc(x2_ready, 1)
                dve.wait_ge(x2_ready, n + 1)
            dve.wait_ge(x2_sq, TA * NH)
            step(V.tensor_tensor(stat[:, VAR2:VAR2 + TA], stat[:, SS2:SS2 + 4:2], stat[:, SS2 + 1:SS2 + 4:2], ALU.add))
            V.tensor_scalar(stat[:, VAR2:VAR2 + TA], stat[:, VAR2:VAR2 + TA], 1.0 / D, EPS, ALU.mult, ALU.add).then_inc(x2_var, 1)
            dve.wait_ge(x2_std, 1)
            step(V.reciprocal(stat[:, RST2:RST2 + TA], stat[:, STD2:STD2 + TA]))
            for h in range(NH):
                cs = slice(h * HALF, (h + 1) * HALF)
                dve.wait_ge(fs_done, h + 1)
                dve.wait_ge(fh_done, h + 1)
                for a in range(TA):
                    step(V.scalar_tensor_tensor(HV[:, a, cs], x_sb[:, a, cs], stat[:, RST2 + a:RST2 + a + 1], B[6 + h][:, :], ALU.mult, ALU.mult))
                    V.tensor_tensor(HV[:, a, cs], HV[:, a, cs], B[4 + h][:, :], ALU.add).then_inc(h2_ready, 1)
            dve.wait_ge(h2T_done, 1)
            for b in (0, 1):
                V.tensor_copy(hT[:, 2 * b:2 * b + 2, :], B[b][:, :].rearrange("p (k t) -> p k t", t=T)).then_inc(h2T_dve, 1)
            dve.wait_ge(part_done, 1)
            V.tensor_copy(part, B[4][:, 0:T]).then_inc(part_ready, 1)
            dve.wait_ge(lg_done, 1)
            dve.wait_ge(s_rw, 32)
            step(V.tensor_tensor(logits, B[5][:, 0:TA * E].rearrange("p (a e) -> p a e", a=TA),
                                 rb.unsqueeze(1).broadcast_to([P, TA, E]), ALU.add))
            for a in range(TA):
                step(V.max(top[:, a, :], logits[:, a, :]))
            V.tensor_scalar(negm, top[:, :, 0], -1.0, None, ALU.mult).then_inc(top_ready, 1)
            for a in range(TA):
                step(V.max_index(topi[:, a, :], top[:, a, :], logits[:, a, :]))
            step(V.tensor_copy(topf, topi))
            oh = onehot.rearrange("p (a j) e -> p a j e", a=TA)
            for a in range(TA):
                step(V.tensor_tensor(oh[:, a], iota[:, 0:E].unsqueeze(1).broadcast_to([P, TOP_K, E]),
                                     topf[:, a, 0:TOP_K].unsqueeze(2).broadcast_to([P, TOP_K, E]), ALU.is_equal))
            for a in range(TA):
                V.tensor_reduce(mask[:, a, :], oh[:, a].rearrange("p j e -> p e j"), AX.X, ALU.add).then_inc(mask_ready, 1)
            dve.wait_ge(exp_done, TA)
            dve.wait_ge(mask_ready, TA)
            step(V.reciprocal(esum, esum))
            step(V.tensor_tensor(topw, topw, esum.unsqueeze(2).broadcast_to([P, TA, TOP_K]), ALU.mult))
            for a in range(TA):
                step(V.tensor_tensor(oh[:, a], oh[:, a], topw[:, a, :].unsqueeze(2).broadcast_to([P, TOP_K, E]), ALU.mult))
            for a in range(TA):
                V.tensor_reduce(wts[:, a, :], oh[:, a].rearrange("p j e -> p e j"), AX.X, ALU.add).then_inc(wts_ready, 1)
            dve.wait_ge(wts_ready, TA)
            V.tensor_copy(wts4.rearrange("p a (r e) -> p a r e", e=E), wts[:, :, :].unsqueeze(2).broadcast_to([P, TA, P // E, E])).then_inc(wts_ready, 1)
            dve.wait_ge(rank_done, 1)
            step(V.scalar_tensor_tensor(pos[:, :, :], B[6][:, 0:TA * E].rearrange("p (a e) -> p a e", a=TA), 1.0, mask, ALU.add, ALU.mult))
            step(V.tensor_scalar(pos[:, :, :], pos[:, :, :], -1.0, None, ALU.add))
            dve.wait_ge(wts_ready, TA)

            def select(e):
                for a in range(TA):
                    V.tensor_scalar(S[:, a, :].rearrange("p (g s) -> p g s", g=NQ), iota[:, :].unsqueeze(1).broadcast_to([P, NQ, CAP]),
                                    pos[:, a, ds(e, 1)], None, ALU.is_equal).then_inc(s_ready, 1)

            def select_weighted(e):
                for a in range(TA):
                    V.tensor_scalar(Sw[:, a, :].rearrange("p (g s) -> p g s", g=NQ), iota[:, :].unsqueeze(1).broadcast_to([P, NQ, CAP]),
                                    pos[:, a, ds(e, 1)], wts[:, a, ds(e, 1)], ALU.is_equal, ALU.mult).then_inc(sw_ready, 1)

            def select_bias(e):
                V.tensor_copy(sel, ident[:, ds(4 * e, 4)].unsqueeze(2).broadcast_to([P, 4, CAP])).then_inc(sel_ready, 1)

            dve.wait_ge(c_iota, 1)
            dve.wait_ge(c_ident, 1)
            select(0)
            step(V.scalar_tensor_tensor(over, B[6][0:1, TA * E:TA * E + E].unsqueeze(2).broadcast_to([1, E, MAXR - 1]), 1.0 / CAP,
                                        iota[0:1, 1:MAXR].unsqueeze(1).broadcast_to([1, E, MAXR - 1]), ALU.mult, ALU.is_gt))
            step(V.tensor_reduce(nover, over, AX.X, ALU.add))
            V.tensor_copy(rounds[:, :], nover).then_inc(table_ready, 1)
            select_weighted(0)
            select_bias(0)
            dve.wait_ge(hTg_done, 1)
            V.tensor_copy(hTg, G[:, 0:QC].rearrange("p (q s) -> p q s", q=KQ)).then_inc(hTg_ready, 1)
            rnd = dve.alloc_register("dve_round")
            dve.reg_mov(rnd, 0)
            dve.wait_ge(table_ready, 1)

            def one_round(e, follower, last=False):
                n = dve.snap(rnd, min_val=0, max_val=ALL_ROUNDS)
                if not last:
                    dve.wait_ge(sw_ready, TA * n + TA)
                    V.tensor_scalar(pos[:, :, ds(e, 1)], pos[:, :, ds(e, 1)], -float(CAP), None, ALU.add).then_inc(pos_moved, 1)
                    dve.wait_ge(gathered, n + 1)
                    dve.wait_ge(pos_moved, n + 1)
                    select(follower)
                dve.wait_ge(gate_done, n + 1)
                V.tensor_scalar(gs, G[:, 0:QC], LIMIT, None, ALU.min).then_inc(gmin_ready, 1)
                dve.wait_ge(sig_ready, n + 1)
                V.tensor_tensor(gs, gs, sg, ALU.mult).then_inc(gs_ready, 1)
                dve.wait_ge(up_done, n + 1)
                V.tensor_scalar(ua, Ub[:, 0:QC], LIMIT, -LIMIT, ALU.min, ALU.max).then_inc(clip_done, 1)
                dve.wait_ge(gs_ready, n + 1)
                dve.wait_ge(clip_done, n + 1)
                V.scalar_tensor_tensor(ua, ua, 1.0, gs, ALU.add, ALU.mult).then_inc(act_ready, 1)
                if not last:
                    dve.wait_ge(hTg_done, n + 2)
                    V.tensor_copy(hTg, G[:, 0:QC].rearrange("p (q s) -> p q s", q=KQ)).then_inc(hTg_ready, 1)
                    dve.wait_ge(swT_done, n + 1)
                    select_weighted(follower)
                    if follower is not e:
                        select_bias(follower)
                dve.wait_ge(swT_ready, n + 2)
                V.tensor_scalar(ST, SwT, 0.0, None, ALU.not_equal).then_inc(st_ready, 1)
                dve.wait_ge(yw_ready, n + 2)
                V.tensor_copy(yp[:, 0, :], yw).then_inc(y_cut, 1)
                dve.wait_ge(y_cut, 2 * n + 1)
                V.tensor_tensor(yr, yw, yp[:, 0, :], ALU.subtract).then_inc(y_rest, 1)
                dve.wait_ge(y_rest, n + 1)
                V.tensor_copy(yp[:, 1, :], yr).then_inc(y_cut, 1)
                dve.wait_ge(y_cut, 2 * n + 2)
                V.tensor_tensor(yp[:, 2, :], yr, yp[:, 1, :], ALU.subtract).then_inc(y_ready, 1)
                dve.reg_add(rnd, rnd, 1)

            def expert(e, last=False):
                more = dve.value_load(rounds[0:1, ds(e, 1)], min_val=0, max_val=MAXR - 1)
                with dve.If(more > 0):
                    with dve.Fori(0, more):
                        one_round(e, e)
                one_round(e, e + 1, last)

            with dve.Fori(0, TURNS) as i:
                for r in range(TURN):
                    expert(TURN * i + r)
            expert(E - 2)
            expert(E - 1, last=True)

            dve.wait_ge(y_all, 1)
            for a in range(TA):
                for g in range(NQ):
                    cs = slice(g * QC, (g + 1) * QC)
                    dve.wait_ge(gf_sb, NH if a else g * QC // HALF + 1)
                    step(V.tensor_tensor(HV[:, 1, cs], Yb[g][:, a * QC:(a + 1) * QC], HV[:, 0, cs], ALU.mult))
                    ins = V.tensor_tensor(x_sb[:, a, cs], x_sb[:, a, cs], HV[:, 1, cs], ALU.add)
                    if g % 2:
                        ins.then_inc(x3_ready, 1)
                        dve.wait_ge(x3_ready, NH * a + g // 2 + 1)
                    else:
                        step(ins)
            for a in range(TA):
                v, s_ = stat[:, VAR3 + a:VAR3 + a + 1], SS3 + 2 * a
                dve.wait_ge(x3_sq, NH * (a + 1))
                step(V.tensor_tensor(v, stat[:, s_:s_ + 1], stat[:, s_ + 1:s_ + 2], ALU.add))
                V.tensor_scalar(v, v, 1.0 / D, EPS, ALU.mult, ALU.add).then_inc(x3_var, 1)
                dve.wait_ge(x3_std, a + 1)
                step(V.reciprocal(stat[:, RST3 + a:RST3 + a + 1], stat[:, STD3 + a:STD3 + a + 1]))
                dve.wait_ge(s_gfin, 16)
                for h in range(NH):
                    cs = slice(h * HALF, (h + 1) * HALF)
                    V.scalar_tensor_tensor(x_sb[:, a, cs], x_sb[:, a, cs], stat[:, RST3 + a:RST3 + a + 1],
                                           gfin[:, cs], ALU.mult, ALU.mult).then_inc(o_ready, 1)

        @block.tensor
        def _(pe):
            M = nc.tensor.matmul
            TR = nc.tensor.transpose

            def arrived(n):
                pe.wait_ge(s_slot[n % RING], 16 * (n // RING + 1))

            pe.wait_ge(c_ident, 1)
            pe.wait_ge(s_rows, 48)
            TR(B[6][:, 0:5 * KT], rows, ident[0:5 * KT, 0:5 * KT]).then_inc(rowsT_done, 1)
            pe.wait_ge(xn_ready, TA)
            for k in range(KT):
                for a in range(TA):
                    c = T * (k % 2) + P * a
                    t = TR(B[k // 2][:, c:c + P], HV[:, a, k * P:(k + 1) * P], ident[:, :])
            t.then_inc(xnT_done, 1)

            def modulation(i):
                if i == 0:
                    pe.wait_ge(cond_ready, 1)
                if i == 1:
                    pe.wait_ge(scale_ready, 1)
                if i == 2:
                    pe.wait_ge(mod_ready, 2)
                for q in range(4):
                    n = unit_no[("ada", i, q)]
                    arrived(n)
                    w = slot(n % RING).rearrange("p (k n) -> p k n", k=2)
                    for kk in range(2):
                        for j in range(4):
                            t = M(B[7][32 * j:32 * j + 32, :], cond[:, 2 * q + kk, :], w[:, kk, HALF * j:HALF * (j + 1)],
                                  start=(q + kk == 0), stop=(q == 3 and kk == 1))
                    t.then_inc(unit_used, 1)
                pe.wait_ge(unit_used, unit_no[("ada", i, 3)] + 1)
                pe.nop().then_inc(ada_done, 1)

            modulation(0)
            pe.wait_ge(mod_ready, 1)
            for q in range(QW):
                t = TR(B[7][:, P * q:P * q + P], mod[:, 0, P * q:P * q + P], ident[:, :])
            t.then_inc(modT_done, 1)
            pe.wait_ge(hT_dve, KT // 2)
            pe.wait_ge(hT_act, KT // 2)
            for h in range(NH):
                n = unit_no[("in", V_, h)]
                arrived(n)
                w = slot(n % RING).rearrange("p (k n) -> p k n", k=KT)
                if h == 1:
                    pe.wait_ge(scale_ready, 1)
                for a in range(TA):
                    for k in range(KT):
                        t = M(B[4 + 2 * h + a][:, :], hT[:, k, a * P:(a + 1) * P], w[:, k, :], start=(k == 0), stop=(k == KT - 1))
                    t.then_inc(v_done, 1)
                pe.wait_ge(v_done, TA * (h + 1))
                pe.nop().then_inc(unit_used, 1)

            pe.wait_ge(ws_masked, 1)
            for g in range(NG):
                t = TR(B[2 + g // 4][:, P * (g % 4):P * (g % 4) + P], ws_nat[:, g, :], ident[:, :])
            t.then_inc(wsT_done, 1)

            def spatial(c):
                if c == 0:
                    pe.wait_ge(v_ready, TA)
                    pe.wait_ge(v_gelu, TA * NH)
                else:
                    pe.wait_ge(sp_used, c)
                for g in (2 * c, 2 * c + 1):
                    for a in range(TA):
                        o = T * (g % 2) + P * a
                        t = M(B[6][:, o:o + P], HV[:, a, g * P:(g + 1) * P], wsT[:, g, :], start=True, stop=True)
                t.then_inc(sp_done, 1)

            for h in range(NH):
                for i, s in enumerate(SECTIONS):
                    n = unit_no[("in", s, h)]
                    arrived(n)
                    w = slot(n % RING).rearrange("p (k n) -> p k n", k=KT)
                    for b in range(2):
                        m = 2 * (NS * h + i) + b
                        if m == 2:
                            pe.wait_ge(wsT_ready, 2)
                        if m >= 4 and m < 6:
                            pe.wait_ge(v_gelu, m - 3)
                        if m >= 6:
                            m0 = m - 6
                            h0, s0, b0 = m0 // (2 * NS), SECTIONS[(m0 // 2) % NS], m0 % 2
                            if s0 in (SC_X, SC_B):
                                pe.wait_ge(sec_dve, dve_bank(h0, s0, b0))
                            else:
                                pe.wait_ge(sec_act, act_bank(h0, s0, b0))
                        for tt in range(2):
                            for k in range(KT):
                                c0 = P * (2 * b + tt)
                                t = M(B[m % 6][:, T * tt:T * tt + T], w[:, k, c0:c0 + P], hT[:, k, :],
                                      start=(k == 0), stop=(k == KT - 1))
                        t.then_inc(sec_done, 1)
                        if s == U_:
                            spatial(2 * h + b)
                    pe.wait_ge(sec_done, 2 * (NS * h + i) + 2)
                    pe.nop().then_inc(unit_used, 1)
                modulation(1 + h)

            def spread(dst, i, j, signal):
                M(dst[:, :], ident[:, 32 * j:32 * j + 1].broadcast_to([P, P]), mod[:, i, :], start=True, stop=True).then_inc(signal, 1)

            pe.wait_ge(c_late, 1)
            pe.wait_ge(mod_ready, 2)
            pe.wait_ge(sec_act, act_bank(NH - 1, GATE_B, 1))
            pe.wait_ge(sec_dve, dve_bank(NH - 1, SC_B, 1))
            pe.wait_ge(sp_used, NG // 2)
            for j in range(NH):
                spread(B[4 + j], 1, j, gm_done)
            pe.wait_ge(m_ready, NH * NH)
            for h in range(NH):
                n = unit_no[("out", 0, h)]
                arrived(n)
                w = slot(n % RING).rearrange("p (k n) -> p k n", k=KT)
                for a in range(TA):
                    for k in range(KT):
                        t = M(B[TA * h + a][:, :], mT[:, k, a * P:(a + 1) * P], w[:, k, :], start=(k == 0), stop=(k == KT - 1))
                    t.then_inc(mix_done, 1)
                pe.wait_ge(mix_done, TA * (h + 1))
                pe.nop().then_inc(unit_used, 1)
                if h == 0:
                    pe.wait_ge(fs_row, 1)
                    for j in range(NH):
                        spread(B[6 + j], 2, j, fs_done)
                    pe.wait_ge(gm_sb, NH)
                    for j in range(NH):
                        spread(B[4 + j], 1, 2 + j, fh_done)
            pe.wait_ge(x2_ready, TA * NH)
            for k in range(KT):
                pe.wait_ge(h2_ready, TA if k < KT // 2 else TA * NH)
                for a in range(TA):
                    c = T * (k % 2) + P * a
                    t = TR(B[k // 2][:, c:c + P], HV[:, a, k * P:(k + 1) * P], ident[:, :])
                if k % 4 == 3:
                    t.then_inc(h2T_done, 1)
            pe.wait_ge(s_rw, 32)
            pe.wait_ge(h2T_dve, 2)
            for k in range(KT):
                if k == 4:
                    pe.wait_ge(h2T_act, 2)
                j = k % 4
                t = M(B[4][32 * j:32 * j + 32, 0:T], rw[:, k, :], hT[:, k, :], start=(k < 4), stop=(k >= 4))
            t.then_inc(part_done, 1)
            pe.wait_ge(part_ready, 1)
            for a in range(TA):
                t = M(B[5][:, a * E:(a + 1) * E], part[:, a * P:(a + 1) * P], stack, start=True, stop=True)
            t.then_inc(lg_done, 1)
            pe.wait_ge(mask_ready, TA)
            M(B[6][:, 0:E], below, mask[:, 0, :], start=True, stop=True)
            M(B[6][:, E:2 * E], below, mask[:, 1, :], start=True, stop=False)
            M(B[6][:, E:2 * E], ones, mask[:, 0, :], start=False, stop=True)
            M(B[6][:, 2 * E:3 * E], ones, mask[:, 0, :], start=True, stop=False)
            M(B[6][:, 2 * E:3 * E], ones, mask[:, 1, :], start=False, stop=True).then_inc(rank_done, 1)
            pe.wait_ge(table_ready, 1)
            pe.wait_ge(s_ready, TA)

            def gather():
                for a in range(TA):
                    for g in range(NQ):
                        t = M(Db[CAP * g:CAP * g + CAP, 0:QC], S[:, a, CAP * g:CAP * g + CAP], HV[:, a, g * QC:(g + 1) * QC],
                              start=(a == 0), stop=(a == TA - 1))
                t.then_inc(gathered, 1)

            def turn(dst, src, signal):
                for q in range(KQ):
                    t = TR(dst[:, P * q:P * q + P], src[:, P * q:P * q + P], ident[:, :])
                t.then_inc(signal, 1)

            gather()
            pe.wait_ge(wts_ready, TA + 1)
            for a in range(TA):
                t = TR(B[7][:, a * P:(a + 1) * P], wts4[:, a, :], ident[:, :])
            t.then_inc(wT_done, 1)
            pe.wait_ge(wT_ready, 1)
            pe.wait_ge(s_bdn, 16)
            pe.wait_ge(dn_zero, 1)
            for g in range(NQ):
                for a in range(TA):
                    t = M(Yb[g][:, a * QC:(a + 1) * QC], wT[:, a * P:(a + 1) * P], b_dn[:, g * QC:(g + 1) * QC],
                          start=(a == 0), stop=True, skip_group_check=True)
            t.then_inc(y_open, 1)
            pe.wait_ge(hg_ready, 1)
            turn(G, hg, hTg_done)
            pe.wait_ge(y_zero, 2)
            pe.wait_ge(s_bgu, 16)
            rnd = pe.alloc_register("pe_round")
            pe.reg_mov(rnd, 0)

            def stream(dst, src, b, uses, first):
                for k in range(KT):
                    if k % 2 == 0:
                        pe.wait_ge(s_block[b % PAIRS][k // 2], 16 * uses)
                    for g in range(NQ):
                        t = M(dst[CAP * g:CAP * g + CAP, 0:QC], src[:, k % KQ, CAP * (k // KQ):CAP * (k // KQ) + CAP],
                              w_half(block_slot(b), k)[:, g * QC:(g + 1) * QC], start=(first and k == 0), stop=(k == KT - 1))
                return t

            def bias(dst, j0):
                ts = [M(dst[CAP * g:CAP * g + CAP, 0:QC], sel[:, j0 + g // 2, :], b_gu[:, QC * (g % 2):QC * (g % 2) + QC],
                        start=True, stop=False) for g in range(NQ)]
                return ts[0]

            def scatter():
                for a in range(TA):
                    for m in range(PARTS):
                        for g in range(NQ):
                            rows_ = slice(CAP * g, CAP * g + CAP)
                            t = M(Yb[g][:, a * QC:(a + 1) * QC], ST[rows_, a * P:(a + 1) * P], yp[rows_, m, :],
                                  start=False, stop=True, skip_group_check=True)
                return t

            def one_round(e, b, turns, done, last=False):
                n = pe.snap(rnd, min_val=0, max_val=ALL_ROUNDS)
                uses = [3 * turns + block_uses(b + i) for i in range(3)]
                pe.wait_ge(sel_ready, e + 1)
                pe.wait_ge(hTg_ready, n + 1)
                bias(G, 0)
                stream(G, hTg, b + GATE, uses[GATE], False).then_inc(gate_done, 1)
                pe.wait_ge(swT_ready, n + 1)
                t = bias(Ub, 2)
                if done:
                    t.then_inc(released, 1)
                stream(Ub, hTg, b + UP, uses[UP], False).then_inc(up_done, 1)
                if not last:
                    pe.wait_ge(yw_ready, n + 1)
                    pe.wait_ge(s_ready, TA * n + 2 * TA)
                    gather()
                pe.wait_ge(y_ready, n + 1)
                pe.wait_ge(st_ready, n + 1)
                t = scatter()
                if done:
                    t.then_inc(released, 1)
                pe.wait_ge(act_ready, n + 1)
                turn(Xb, ua, actT_done)
                if not last:
                    pe.wait_ge(hg_ready, n + 2)
                    turn(G, hg, hTg_done)
                pe.wait_ge(sw_ready, TA * n + TA)
                for a in range(TA):
                    t = TR(Ub[:, a * P:(a + 1) * P], Sw[:, a, :], ident[:, :])
                t.then_inc(swT_done, 1)
                pe.wait_ge(actT_ready, n + 1)
                stream(Db, actT, b + DOWN, uses[DOWN], True).then_inc(down_done, 1)
                if done:
                    pe.wait_ge(down_done, n + 1)
                    pe.nop().then_inc(released, 1)
                pe.reg_add(rnd, rnd, 1)

            def expert(e, b, turns, last=False):
                more = pe.value_load(rounds[0:1, ds(e, 1)], min_val=0, max_val=MAXR - 1)
                with pe.If(more > 0):
                    with pe.Fori(0, more):
                        one_round(e, b, turns, False)
                one_round(e, b, turns, True, last)

            with pe.Fori(0, TURNS) as i:
                for r in range(TURN):
                    expert(TURN * i + r, 3 * r, i)
            expert(E - 2, 0, TURNS)
            expert(E - 1, 3, TURNS, last=True)
            n = pe.snap(rnd, min_val=0, max_val=ALL_ROUNDS)
            pe.wait_ge(swT_ready, n + 1)
            for j in range(NH):
                spread(B[4 + j], 2, 2 + j, gf_done)
            pe.wait_ge(y_ready, n + 1)
            pe.wait_ge(st_ready, n + 1)
            scatter().then_inc(y_all, 1)


_INS = ["x", "c", "w_ada", "b_ada", "norm_mix_g", "w_in", "conv_w", "w_spatial", "b_spatial", "ln_v_g",
        "w_out", "norm_ffn_g", "router_w", "router_b", "w_gate_up", "b_gate_up", "w_down", "b_down",
        "final_norm_g"]


def kernel(**inputs):
    import numpy as _np
    import concourse.bacc as _bacc
    from concourse import mybir as _mybir
    from concourse.bass_utils import run_bass_kernel_spmd as _run

    nc = _bacc.Bacc("TRN2", target_bir_lowering=False, num_devices=1)
    arrays, args = {}, []
    for name in _INS:
        a = _np.ascontiguousarray(inputs[name])
        arrays[f"in_{name}_dram"] = a
        args.append(nc.dram_tensor(f"in_{name}_dram", a.shape, _mybir.dt.from_np(a.dtype), kind="ExternalInput").ap())
    shape = tuple(inputs["x"].shape)
    args.append(nc.dram_tensor("out_0_dram", shape, _mybir.dt.float32, kind="ExternalOutput").ap())
    hybrid_trunk(nc, *args)
    r = _run(nc, [arrays], core_ids=[0])
    return r.results[0]["out_0_dram"]
```

```python
import concourse.bass as bass
from concourse import mybir
from contextlib import ExitStack


def hybrid_trunk(nc, x_in, c_in, w_ada, b_ada, norm_mix_g, w_in, conv_w, w_spatial, b_spatial, ln_v_g,
                 w_out, norm_ffn_g, router_w, router_b, w_gate_up, b_gate_up, w_down, b_down,
                 final_norm_g, out):
    f32r = mybir.dt.float32r
    f32, i32, u32, bf16 = mybir.dt.float32, mybir.dt.int32, mybir.dt.uint32, mybir.dt.bfloat16
    ALU, ACT, AX = mybir.AluOpType, mybir.ActivationFunctionType, mybir.AxisListType
    ds = bass.ds

    P = 128
    DEPTH, D, D_IN = w_in.shape
    T = x_in.shape[1]
    E = router_w.shape[2]
    FF = w_down.shape[2]
    NG = w_spatial.shape[1]
    TOP_K = 4
    LIMIT, ALPHA, EPS = 7.0, 1.702, 1e-6
    TA = T // P
    KT = D // P
    HALF = 512
    NH = D // HALF
    CAP = 32
    MAXR = T // CAP
    NQ = P // CAP
    QC = D // NQ
    KQ = QC // P
    ALL_ROUNDS = T * TOP_K // CAP + E
    PARTS = 3
    QW = HALF // P
    assert DEPTH == 1 and T == 2 * P and D == 2 * HALF and FF == D and NG == KT and E == 32

    SC_X, SC_B, SC_C, U_, V_, GATE_A, GATE_B = range(7)
    SECTIONS = [SC_C, SC_X, SC_B, GATE_A, U_, GATE_B]
    NS = len(SECTIONS)

    UW = KT * HALF
    RING = 3
    SLOTS = 10
    SPLITS = 2
    units = [("ada", 0, q) for q in range(4)] + [("in", V_, h) for h in range(NH)]
    for h in range(NH):
        for i, s in enumerate(SECTIONS):
            units.append(("in", s, h))
            if i < 4:
                units.append(("ada", 1 + h, i))
    units += [("out", 0, h) for h in range(NH)]
    split_units = [n for n, u in enumerate(units) if u[0] != "ada"]
    ada_units = [n for n, u in enumerate(units) if u[0] == "ada"]
    unit_no = {u: n for n, u in enumerate(units)}
    NU = len(units)

    ctx = ExitStack()
    with ctx:
        def sb(name, shape, dt=f32):
            return ctx.enter_context(nc.sbuf_tensor(name, shape, dt))

        def sem(name):
            return ctx.enter_context(nc.semaphore(name))

        with ExitStack() as early:
            def sb1(name, shape, dt=f32):
                return early.enter_context(nc.sbuf_tensor(name, shape, dt))

            raw = sb1("raw", [P, RING * UW])
            wh, wl = [], []
            for r in range(2):
                wh.append(sb1(f"wh{r}", [P, KT, HALF], f32r))
                wl.append(sb1(f"wl{r}", [P, KT, HALF], f32r))
            mh = sb1("mh", [P, KT, T], f32r)
            ml = sb1("ml", [P, KT, T], f32r)
            tmp = sb1("tmp", [P, 2 * UW])
            hh = sb1("hh", [P, KT, T], f32r)
            hl = sb1("hl", [P, KT, T], f32r)
        W = sb("W", [P, SLOTS * UW])
        hT = sb("hT", [P, KT, T])
        mT = sb("mT", [P, KT, T])
        x_sb = sb("x_sb", [P, TA, D])
        HV = sb("HV", [P, TA, D])
        mod = sb("mod", [P, 3, HALF])
        EW = sb("EW", [P, 3 * HALF])
        b_gu = sb("b_gu", [P, HALF])
        ident = sb("ident", [P, P])
        iota = sb("iota", [P, CAP])
        pos = sb("pos", [P, TA, E])
        wts = sb("wts", [P, TA, E])
        cols = sb("cols", [P, 5 * KT])
        stat = sb("stat", [P, 64])
        rounds = sb("rounds", [1, E], i32)

        def slot(n, k=1):
            return W[:, n * UW:(n + k) * UW]

        accA = tmp[:, 0:D].rearrange("p (t n) -> p t n", n=T)
        accB = tmp[:, D:2 * D].rearrange("p (t n) -> p t n", n=T)
        accC = tmp[:, 2 * D:3 * D].rearrange("p (t n) -> p t n", n=T)
        ws_nat = tmp[:, 0:D].rearrange("p (g s) -> p g s", g=NG)
        bs_all = tmp[:, 3 * D:4 * D].rearrange("p (g t) -> p g t", g=NG)
        wsT = tmp[:, 4 * D:5 * D].rearrange("p (g t) -> p g t", g=NG)
        lng = tmp[:, 5 * D:6 * D]
        late = tmp[:, 6 * D:8 * D]
        below = late[:, 0:P // 2].bitcast(bf16)
        ones = late[:, P:P + P // 2].bitcast(bf16)
        rw = late[:, 3 * P:3 * P + KT * E].rearrange("p (k e) -> p k e", k=KT)
        cond = late[:, 5 * P:5 * P + KT * 32].rearrange("p (k r) -> p k r", k=KT)
        stack = late[:, 7 * P:7 * P + E]
        rb = late[:, 7 * P + E:7 * P + 2 * E]
        cT = late[:, 7 * P + 2 * E:7 * P + 2 * E + KT]
        shm = late[:, 7 * P + 2 * E + KT:7 * P + 2 * E + 2 * KT]
        scm = late[:, 7 * P + 2 * E + 2 * KT:7 * P + 2 * E + 3 * KT]
        sig = late[:, 8 * P:8 * P + HALF]
        stmp = late[:, 8 * P + HALF:8 * P + 2 * HALF]
        junk = [tmp[:, D:2 * D], tmp[:, 2 * D:3 * D]]
        hf = tmp[:, D:3 * D].rearrange("p (k t) -> p k t", t=T)
        rows = EW[0:5 * KT, HALF:HALF + P]
        gffn = EW[0:64, 2 * HALF:3 * HALF]
        gffn_all = EW[:, 2 * HALF:3 * HALF]
        gate = [sig, stmp]
        b_dn = EW[:, 0:2 * HALF]
        part = EW[:, 2 * HALF:2 * HALF + T]
        wT = EW[:, 2 * HALF + T:2 * HALF + 2 * T]
        onehot = mod[:, 0, 0:8 * E].rearrange("p (n e) -> p n e", e=E)
        logits = mod[:, 0, 8 * E:10 * E].rearrange("p (a e) -> p a e", a=TA)
        mask = mod[:, 0, 10 * E:11 * E].bitcast(bf16).rearrange("p (a e) -> p a e", a=TA)
        top = mod[:, 0, 12 * E:12 * E + 16].rearrange("p (a j) -> p a j", a=TA)
        topi = mod[:, 0, 12 * E + 16:12 * E + 32].bitcast(u32).rearrange("p (a j) -> p a j", a=TA)
        topf = mod[:, 0, 12 * E + 32:12 * E + 48].rearrange("p (a j) -> p a j", a=TA)
        topw = mod[:, 0, 12 * E + 48:12 * E + 56].rearrange("p (a j) -> p a j", a=TA)
        negm = mod[:, 0, 12 * E + 56:12 * E + 58]
        esum = mod[:, 0, 12 * E + 58:12 * E + 60]
        shl = mod[:, 0, 12 * E + 64:13 * E + 64]
        over = mod[0:1, 0, 0:E * (MAXR - 1)].rearrange("p (e m) -> p e m", e=E)
        nover = mod[0:1, 0, E * (MAXR - 1):E * MAXR]

        def w_half(n, rows_):
            return slot(n, 2).rearrange("p (k n) -> p k n", k=KT)[:, rows_, :]

        PAIRS = SLOTS // 2
        QUARTERS = 4
        GATE, UP, DOWN = range(3)
        TURN = PAIRS
        TURNS = (E - 2) // TURN
        assert TURNS * TURN + 2 == E

        def block_slot(b):
            return 2 * (0, 4, 1, 2, 3)[b % PAIRS]

        def block_uses(b):
            return b // PAIRS + 1

        work = mT[:, :, :].rearrange("p k t -> p (k t)")
        S = work[:, 0:256].rearrange("p (a s) -> p a s", a=TA)
        Sw = work[:, 256:512].rearrange("p (a s) -> p a s", a=TA)
        SwT = work[:, 512:512 + T]
        hg = work[:, 768:768 + QC]
        hTg = work[:, 1024:1024 + QC].rearrange("p (q s) -> p q s", q=KQ)
        actT = work[:, 1280:1280 + QC].rearrange("p (q s) -> p q s", q=KQ)
        wts4 = work[:, 1280:1280 + TA * P].rearrange("p (a n) -> p a n", a=TA)
        sel = work[:, 1536:1536 + P].rearrange("p (j s) -> p j s", j=4)
        work2 = hT[:, :, :].rearrange("p k t -> p (k t)")
        gfq = work[:, 1664:1664 + QC]
        yw = work2[:, 0:QC]
        yr = work2[:, QC:2 * QC]
        yp = work2[:, 2 * QC:3 * QC].bitcast(bf16).rearrange("p (m n) -> p m n", m=2)
        ST = work2[:, 4 * QC:4 * QC + T // 2].bitcast(bf16)
        ys = work2[0:PARTS * CAP, 5 * QC:7 * QC].bitcast(bf16)
        gs, sg, ua = EW[:, 0:QC], EW[:, HALF:HALF + QC], EW[:, 2 * HALF:2 * HALF + QC]

        gfin = slot(block_slot(3 * (E - 2) + UP))[:, 0:D]

        B = [ctx.enter_context(nc.psum_tensor(f"B{n}", [P, HALF], f32)) for n in range(8)]
        Yb = [B[0:NH], B[NH:2 * NH]]
        G, Ub, Db, Xb = B[4], B[5], B[6], B[7]
        ranks = B[4][:, 0:3 * E]

        s_x = sem("s_x"); s_rows = sem("s_rows"); s_bada = sem("s_bada"); s_bada_rest = sem("s_bada_rest"); s_first = sem("s_first"); s_gffn = sem("s_gffn")
        s_ws = sem("s_ws"); s_bs = sem("s_bs"); s_lng = sem("s_lng"); s_rw = sem("s_rw")
        s_bgu = sem("s_bgu"); s_bdn = sem("s_bdn"); s_gfin = sem("s_gfin"); s_out = sem("s_out")
        s_slot = [sem(f"s_slot{n}") for n in range(RING)]
        ada_used = sem("ada_used"); split_h = sem("split_h"); split_l = sem("split_l")
        c_ident = sem("c_ident"); c_iota = sem("c_iota"); c_late = sem("c_late"); pool_step = sem("pool_step")
        ws_masked = sem("ws_masked")
        dve_step = sem("dve_step")
        act_step = sem("act_step")
        x_sq = sem("x_sq"); x_var = sem("x_var"); x_std = sem("x_std"); xn_ready = sem("xn_ready")
        xnT_done = sem("xnT_done"); rowsT_done = sem("rowsT_done"); cols_ready = sem("cols_ready")
        silu_done = sem("silu_done"); cond_ready = sem("cond_ready")
        mod_ready = sem("mod_ready"); modT_done = sem("modT_done")
        scale_ready = sem("scale_ready"); hT_act = sem("hT_act"); hT_dve = sem("hT_dve")
        wsT_done = sem("wsT_done"); wsT_ready = sem("wsT_ready")
        v_done = sem("v_done"); v_gelu = sem("v_gelu"); v_mu = sem("v_mu"); v_sq = sem("v_sq")
        v_var = sem("v_var"); v_std = sem("v_std"); v_ready = sem("v_ready")
        sec_done = sem("sec_done")
        sec_act = sem("sec_act")
        sec_dve = sem("sec_dve")
        sp_done = sem("sp_done"); sp_used = sem("sp_used"); m_sum = sem("m_sum"); mh_ready = sem("mh_ready"); m_ready = sem("m_ready")
        hh_ready = sem("hh_ready"); hl_ready = sem("hl_ready")
        mix_done = sem("mix_done"); gm_sb = sem("gm_sb")
        x2_ready = sem("x2_ready"); xs_ready = sem("xs_ready"); x2_sq = sem("x2_sq"); x2_var = sem("x2_var"); x2_std = sem("x2_std")
        fs_row = sem("fs_row"); fs_done = sem("fs_done"); fh_done = sem("fh_done")
        fhT_done = sem("fhT_done"); fhT_ready = sem("fhT_ready"); shl_done = sem("shl_done"); shl_ready = sem("shl_ready"); h2_ready = sem("h2_ready"); h2T_done = sem("h2T_done"); h2T_act = sem("h2T_act"); h2T_dve = sem("h2T_dve")
        part_done = sem("part_done"); part_ready = sem("part_ready"); lg_done = sem("lg_done")
        top_ready = sem("top_ready"); exp_done = sem("exp_done"); mask_ready = sem("mask_ready")
        wts_ready = sem("wts_ready"); rank_done = sem("rank_done"); wT_done = sem("wT_done")
        wT_ready = sem("wT_ready"); table_ready = sem("table_ready"); y_zero = sem("y_zero"); pos_moved = sem("pos_moved");
        dn_zero = sem("dn_zero"); yw_ready = sem("yw_ready"); st_ready = sem("st_ready"); y_cut = sem("y_cut"); y_rest = sem("y_rest"); y_moved = sem("y_moved"); y_low = sem("y_low"); gf_used = sem("gf_used")
        s_block = [[sem(f"s_block{r}{q}") for q in range(4)] for r in range(PAIRS)]
        s_ready = sem("s_ready"); sw_ready = sem("sw_ready"); sel_ready = sem("sel_ready")
        gathered = sem("gathered"); hg_ready = sem("hg_ready"); hTg_done = sem("hTg_done")
        hTg_ready = sem("hTg_ready"); gate_done = sem("gate_done"); gmin_ready = sem("gmin_ready")
        sig_ready = sem("sig_ready"); gs_ready = sem("gs_ready"); swT_done = sem("swT_done")
        swT_ready = sem("swT_ready"); up_done = sem("up_done"); clip_done = sem("clip_done")
        act_ready = sem("act_ready"); actT_done = sem("actT_done"); actT_ready = sem("actT_ready")
        down_done = sem("down_done"); released = sem("released")
        y_all = sem("y_all"); x3_sq = sem("x3_sq"); x3_var = sem("x3_var"); x3_std = sem("x3_std"); o_ready = sem("o_ready"); xg_ready = sem("xg_ready"); oa_ready = sem("oa_ready"); rst_ready = sem("rst_ready")

        ba = b_ada[0].rearrange("(i j n) -> j i n", i=3, j=4)
        ada_v = w_ada[0].rearrange("(q k p) n -> q p k n", k=2, p=P)
        in_v = w_in[0].rearrange("(k p) n -> p k n", p=P)
        out_v = w_out[0].rearrange("(k p) n -> p k n", p=P)
        gu_v = w_gate_up[0].rearrange("e (q k p) n -> e q p k n", k=2, p=P)
        dn_v = w_down[0].rearrange("e (q k p) n -> e q p k n", k=2, p=P)

        SS, VAR, STD, RST = 0, 4, 6, 8
        VS, NMU, VSS, VVAR, VSTD, VRST = 10, 14, 16, 18, 20, 22
        SS2, VAR2, STD2, RST2 = 24, 30, 32, 34
        SS3, VAR3, STD3, RST3 = 36, 42, 44, 46
        WSL = 48
        WARM = 49

        dve_order = [(h, s, b) for h in range(NH) for s in SECTIONS if s not in (SC_C, U_) for b in range(2)]

        def dve_bank(h, s, b):
            return dve_order.index((h, s, b)) + 1

        act_order = [(h, s, b) for h in range(NH) for s in SECTIONS if s in (SC_C, GATE_A, U_, GATE_B) for b in range(2)]

        def act_bank(h, s, b):
            return act_order.index((h, s, b)) + 1

        def raw_slot(n):
            return raw[:, (n % RING) * UW:(n % RING + 1) * UW]

        def product_done(eng, j):
            if j < NH:
                eng.wait_ge(v_done, TA * (j + 1))
            elif j < NH + NH * NS:
                eng.wait_ge(sec_done, 2 * (j - NH) + 2)
            else:
                eng.wait_ge(mix_done, TA * (j - NH - NH * NS + 1))

        def part_of(t, c):
            k = KT // SPLITS
            return t[:, c * k:(c + 1) * k, :]

        block = ctx.enter_context(nc.Block())

        @block.sync
        def _(sp):
            sp.dma_start(rows[4 * KT:5 * KT, :], c_in[0].rearrange("(k p) -> k p", p=P)).then_inc(s_rows, 16)
            sp.dma_start(rows[0:KT, :], norm_mix_g[0].rearrange("(k p) -> k p", p=P)).then_inc(s_rows, 16)
            sp.dma_start(rows[KT:4 * KT, :], conv_w[0].rearrange("j (k p) -> (j k) p", p=P)).then_inc(s_rows, 16)
            sp.dma_start(x_sb[:, :, :], x_in[0].rearrange("(a p) n -> p a n", p=P)).then_inc(s_x, 16)
            for n, (kind, s, h) in enumerate(units):
                if n >= RING:
                    m = n - RING
                    if m in ada_units:
                        sp.wait_ge(ada_used, ada_units.index(m) + 1)
                    else:
                        sp.wait_ge(split_l, SPLITS * (split_units.index(m) + 1))
                if kind == "ada":
                    src = ada_v[h, :, :, 4 * HALF * s:4 * HALF * (s + 1)]
                    dst = raw_slot(n).rearrange("p (k n) -> p k n", k=2)
                else:
                    c0 = (s * D if kind == "in" else 0) + h * HALF
                    src = (in_v if kind == "in" else out_v)[:, :, c0:c0 + HALF]
                    dst = raw_slot(n).rearrange("p (k n) -> p k n", k=KT)
                if n == split_units[0]:
                    k = KT // SPLITS
                    sp.dma_start(dst[:, 0:k, :], src[:, 0:k, :]).then_inc(s_first, 16)
                    sp.dma_start(dst[:, k:KT, :], src[:, k:KT, :]).then_inc(s_slot[n % RING], 16)
                else:
                    sp.dma_start(dst, src).then_inc(s_slot[n % RING], 16)
                if n == ada_units[3]:
                    for j in range(4):
                        sp.dma_start(mod[32 * j:32 * j + 32, 0, :], ba[j][0].partition_broadcast(32)).then_inc(s_bada, 16)
                if n == split_units[1]:
                    sp.dma_start(ws_nat, w_spatial[0].rearrange("g t s -> t g s")).then_inc(s_ws, 16)
                    sp.dma_start(bs_all, b_spatial[0].partition_broadcast(P)).then_inc(s_bs, 16)
                    sp.dma_start(lng, ln_v_g[0].partition_broadcast(P)).then_inc(s_lng, 16)
                if n == split_units[3]:
                    for j in range(4):
                        sp.dma_start(mod[32 * j:32 * j + 32, 1:3, :], ba[j][1:3].partition_broadcast(32)).then_inc(s_bada_rest, 16)
                if n == split_units[5]:
                    gf = norm_ffn_g[0].rearrange("(j n) -> j n", j=NH)
                    for j in range(NH):
                        sp.dma_start(gffn[32 * j:32 * j + 32, :], gf[j].partition_broadcast(32)).then_inc(s_gffn, 16)
                    sp.dma_start(rw, router_w[0].rearrange("(k p) e -> p k e", p=P)).then_inc(s_rw, 16)
                    sp.dma_start(rb, router_b[0].partition_broadcast(P)).then_inc(s_rw, 16)
                    sp.dma_start(b_gu[:, :], b_gate_up[0].rearrange("e (j n) -> (e j) n", j=4)).then_inc(s_bgu, 16)
                    sp.wait_ge(cols_ready, 1)
                    sp.dma_start(b_dn[0:E, :], b_down[0]).then_inc(s_bdn, 16)

            def load(b, e, qs=range(4)):
                src = (gu_v[e, :, :, :, 0:FF], gu_v[e, :, :, :, FF:2 * FF], dn_v[e, :, :, :, :])[b % 3]
                for q in qs:
                    sp.dma_start(w_half(block_slot(b), slice(2 * q, 2 * q + 2)), src[q]).then_inc(s_block[b % PAIRS][q], 16)

            assert [n % RING for n in (NU - 3, NU - 2, NU - 1)] == [1, 2, 0]
            sp.wait_ge(split_l, SPLITS * (len(split_units) - 2))
            load(0, 0, (2, 3))
            sp.wait_ge(sp_done, NG // 2)
            load(1, 0, (2,))
            sp.wait_ge(split_l, SPLITS * (len(split_units) - 1))
            load(2, 0, (0, 1))
            sp.wait_ge(m_ready, NH * 2)
            load(1, 0, (0, 1))
            sp.wait_ge(split_l, SPLITS * len(split_units))
            load(0, 0, (0, 1))
            sp.wait_ge(mix_done, TA)
            load(2, 0, (2, 3))
            load(3, 1, (0, 1))
            sp.wait_ge(mix_done, TA * NH)
            load(3, 1, (2, 3))
            load(4, 1)
            sp.wait_ge(table_ready, 1)
            load(1, 0, (3,))
            with sp.Fori(0, TURNS) as i:
                for b in range(PAIRS, PAIRS + 3 * TURN):
                    for q in range(QUARTERS):
                        sp.wait_ge(released, QUARTERS * (3 * TURN * i + b - PAIRS) + q + 1)
                        load(b, TURN * i + b // 3, (q,))
            b = 3 * E - 1
            for q in range(QUARTERS):
                sp.wait_ge(released, QUARTERS * (b - PAIRS) + q + 1)
                load(b, E - 1, (q,))
            sp.wait_ge(released, QUARTERS * (3 * (E - 2) + UP + 1))
            sp.dma_start(gfin, final_norm_g[:].partition_broadcast(P)).then_inc(s_gfin, 16)
            for h in range(NH):
                cs = slice(h * HALF, (h + 1) * HALF)
                for a in range(TA):
                    sp.wait_ge((oa_ready, o_ready)[a], h + 1)
                    sp.dma_start(out[0, a * P:(a + 1) * P, cs], HV[:, a, cs]).then_inc(s_out, 16)
            sp.wait_ge(s_out, 16 * TA * NH)

        @block.gpsimd
        def _(pool):
            done = [0]

            def one(ins, signal):
                ins.then_inc(pool_step, 1)
                done[0] += 1
                pool.wait_ge(pool_step, done[0])
                if signal is not None:
                    pool.nop().then_inc(signal, 1)

            G_ = nc.gpsimd
            one(G_.memset(ident[:, :], 0.0), None)
            one(G_.affine_select(out=ident[:, :], in_=ident[:, :], compare_op=ALU.not_equal, fill=1.0,
                                 base=0, pattern=[[-1, P]], channel_multiplier=1), c_ident)
            one(G_.iota(iota[:, :], pattern=[[1, CAP]], base=0, channel_multiplier=0,
                        allow_small_or_imprecise_dtypes=True), c_iota)
            pool.wait_ge(s_ws, 16)
            one(G_.affine_select(out=ws_nat, in_=ws_nat, compare_op=ALU.is_ge, fill=0.0,
                                 base=0, pattern=[[0, NG], [-1, P]], channel_multiplier=1), ws_masked)
            pool.wait_ge(cols_ready, 1)
            one(G_.memset(b_dn[E:2 * E, :], 0.0), None)
            one(G_.memset(b_dn[2 * E:4 * E, :], 0.0), dn_zero)
            one(G_.memset(below, 1.0), None)
            one(G_.affine_select(out=below, in_=below, compare_op=ALU.is_gt, fill=0.0,
                                 base=0, pattern=[[1, P]], channel_multiplier=-1), None)
            one(G_.memset(ones, 1.0), None)
            one(G_.memset(stack, 0.0), None)
            for j in range(4):
                v = stack[32 * j:32 * j + 32, :]
                one(G_.affine_select(out=v, in_=v, compare_op=ALU.not_equal, fill=1.0,
                                     base=0, pattern=[[-1, E]], channel_multiplier=1), c_late if j == 3 else None)
            pool.wait_ge(lg_done, 1)
            one(G_.memset(ys, 0.0), y_zero)
            one(G_.memset(ST, 0.0), y_zero)
            pool.nop().then_inc(yw_ready, 1)
            pool.nop().then_inc(y_moved, 2 * NQ)
            pool.nop().then_inc(y_low, NQ)
            pool.nop().then_inc(swT_ready, 1)
            pool.nop().then_inc(st_ready, 1)

        @block.scalar
        def _(act):
            A = nc.scalar.activation
            act.wait_ge(cols_ready, 1)
            A(cT, cols[:, 4 * KT:5 * KT], ACT.Silu).then_inc(silu_done, 1)
            act.wait_ge(s_x, 16)
            for a in range(TA):
                A(junk[a], x_sb[:, a, :], ACT.Square, accum_out=stat[:, SS + a:SS + a + 1]).then_inc(x_sq, 1)
            act.wait_ge(x_var, 1)
            A(stat[:, STD:STD + TA], stat[:, VAR:VAR + TA], ACT.Sqrt).then_inc(x_std, 1)

            def split_high(j, cs=range(SPLITS)):
                n = split_units[j]
                src = raw_slot(n).rearrange("p (k n) -> p k n", k=KT)
                for c in cs:
                    if j == 0 and c == 0:
                        act.wait_ge(s_first, 16)
                    else:
                        act.wait_ge(s_slot[n % RING], 16 * (n // RING + 1))
                    if j >= 2 and c == 0:
                        product_done(act, j - 2)
                    A(part_of(wh[j % 2], c), part_of(src, c), ACT.Copy).then_inc(split_h, 1)

            split_high(0, (0,))
            act.wait_ge(xnT_done, 1)
            act.wait_ge(scale_ready, 1)
            for k in range(KT // 2, KT):
                A(hf[:, k, :], B[k // 2][:, T * (k % 2):T * (k % 2) + T], ACT.Identity,
                  scale=scm[:, k:k + 1], bias=shm[:, k:k + 1]).then_inc(hT_act, 1)
            act.wait_ge(hT_dve, KT // 2)
            A(part_of(hh, 0), part_of(hf, 0), ACT.Copy).then_inc(hh_ready, 1)
            act.wait_ge(hT_act, KT // 2)
            A(part_of(hh, 1), part_of(hf, 1), ACT.Copy).then_inc(hh_ready, 1)

            split_high(0, (1,))
            split_high(1)
            for h in range(NH):
                split_high(2 + h)
                for a in range(TA):
                    act.wait_ge(v_done, NH * h + a + 1)
                    A(HV[:, a, h * HALF:(h + 1) * HALF], B[4 + 2 * h + a][:, :], ACT.Gelu,
                      accum_out=stat[:, VS + 2 * a + h:VS + 2 * a + h + 1]).then_inc(v_gelu, 1)
            act.wait_ge(v_mu, 1)
            for a in range(TA):
                A(junk[a], HV[:, a, :], ACT.Square, bias=stat[:, NMU + a:NMU + a + 1],
                  accum_out=stat[:, VSS + a:VSS + a + 1]).then_inc(v_sq, 1)
            act.wait_ge(v_var, 1)
            A(stat[:, VSTD:VSTD + TA], stat[:, VVAR:VVAR + TA], ACT.Sqrt).then_inc(v_std, 1)

            def m_high(h, b):
                act.wait_ge(m_sum, 2 * h + b + 1)
                A(mh[:, 4 * h + 2 * b:4 * h + 2 * b + 2, :], accB[:, 2 * b:2 * b + 2, :], ACT.Copy).then_inc(mh_ready, 1)

            for h in range(NH):
                for n, s in enumerate(SECTIONS):
                    for b in range(2):
                        if b == 1 and NS * h + n < NS * NH - 1:
                            split_high(NH + NS * h + n + 2)
                        if b == 1 and s == GATE_B:
                            m_high(h, 0)
                        m = 2 * (NS * h + n) + b
                        bank = B[m % 6][:, :]
                        if s in (SC_X, SC_B):
                            continue
                        act.wait_ge(sec_done, m + 1)
                        if s == SC_C:
                            if h == 0 and b == 0:
                                act.wait_ge(wsT_done, 1)
                            if h > 0:
                                act.wait_ge(m_sum, 2 * (h - 1) + b + 1)
                            A(accA[:, 2 * b:2 * b + 2, :], bank.rearrange("p (t n) -> p t n", n=T), ACT.Copy).then_inc(sec_act, 1)
                        elif s == U_:
                            if h > 0:
                                act.wait_ge(m_sum, 2 * (h - 1) + b + 1)
                            A(accC[:, 2 * b:2 * b + 2, :], bank.rearrange("p (t n) -> p t n", n=T), ACT.Gelu).then_inc(sec_act, 1)
                        else:
                            if s == GATE_A and b == 0 and h > 0:
                                act.wait_ge(sec_dve, dve_bank(h - 1, GATE_B, 1))
                            if s == GATE_A and b == 1:
                                act.wait_ge(sec_dve, dve_bank(h, GATE_A, 0))
                            if s == GATE_B:
                                act.wait_ge(sec_dve, dve_bank(h, GATE_A, 1) if b == 0 else dve_bank(h, GATE_B, 0))
                            A(sig, bank, ACT.Sigmoid).then_inc(sec_act, 1)
                m_high(h, 1)
            split_high(len(split_units) - 1)
            act.wait_ge(mod_ready, 2)
            for h in range(NH):
                for q in range(4):
                    A(gate[h][32 * q:32 * q + 32, :], mod[32 * h:32 * h + 32, 1, :], ACT.Copy).then_inc(gm_sb, 1)
            A(stat[:, WARM:WARM + 1], stat[:, VVAR:VVAR + 1], ACT.Sqrt).then_inc(act_step, 1)
            for n in range(TA * NH):
                act.wait_ge(x2_ready, n + 1)
                a, h = n % TA, n // TA
                A(gffn_all, x_sb[:, a, h * HALF:(h + 1) * HALF], ACT.Square,
                  accum_out=stat[:, SS2 + 2 * a + h:SS2 + 2 * a + h + 1]).then_inc(x2_sq, 1)
                act.wait_ge(x2_sq, n + 1)
                if n == TA - 1:
                    for a2 in range(TA):
                        act.wait_ge(h2T_done, a2 + 1)
                        A(hT[:, 0:QW, a2 * P:(a2 + 1) * P], B[a2][:, :].rearrange("p (k t) -> p k t", t=P), ACT.Copy).then_inc(h2T_act, 1)
            act.wait_ge(x2_var, 1)
            A(stat[:, STD2:STD2 + TA], stat[:, VAR2:VAR2 + TA], ACT.Sqrt).then_inc(x2_std, 1)
            act.wait_ge(h2T_done, 4)
            A(hT[:, QW:KT, P:T], B[3][:, :].rearrange("p (k t) -> p k t", t=P), ACT.Copy).then_inc(h2T_act, 1)
            act.wait_ge(part_done, 1)
            A(part, B[6][:, 0:T], ACT.Copy).then_inc(part_ready, 1)
            act.wait_ge(top_ready, 1)
            for a in range(TA):
                A(topw[:, a, :], top[:, a, 0:TOP_K], ACT.Exp, bias=negm[:, a:a + 1],
                  accum_out=esum[:, a:a + 1]).then_inc(exp_done, 1)
            act.wait_ge(gathered, 1)
            A(hg, Db[:, 0:QC], ACT.Copy).then_inc(hg_ready, 1)
            act.wait_ge(wT_done, 1)
            A(wT, B[7][:, 0:T], ACT.Copy).then_inc(wT_ready, 1)
            rnd = act.alloc_register("act_round")
            act.reg_mov(rnd, 0)

            def one_round(last=False):
                n = act.snap(rnd, min_val=0, max_val=ALL_ROUNDS)
                act.wait_ge(gmin_ready, n + 1)
                A(sg, gs, ACT.Sigmoid, scale=ALPHA).then_inc(sig_ready, 1)
                if not last:
                    act.wait_ge(gathered, n + 2)
                    A(hg, Db[:, 0:QC], ACT.Copy).then_inc(hg_ready, 1)
                act.wait_ge(actT_done, n + 1)
                A(actT, Xb[:, 0:QC].rearrange("p (q s) -> p q s", q=KQ), ACT.Copy).then_inc(actT_ready, 1)
                act.wait_ge(swT_done, n + 1)
                A(SwT, Ub[:, 0:T], ACT.Copy, accum_out=stat[:, WSL:WSL + 1]).then_inc(swT_ready, 1)
                for m in range(2):
                    act.wait_ge(y_cut, 2 * n + m + 1)
                    for g in range(NQ):
                        A(ys[CAP * m:CAP * m + CAP, g * QC:(g + 1) * QC], yp[CAP * g:CAP * g + CAP, m, :], ACT.Copy).then_inc(y_moved, 1)
                act.reg_add(rnd, rnd, 1)

            def expert(e, last=False):
                more = act.value_load(rounds[0:1, ds(e, 1)], min_val=0, max_val=MAXR - 1)
                with act.If(more > 0):
                    with act.Fori(0, more):
                        one_round()
                one_round(last)

            act.wait_ge(table_ready, 1)
            with act.Fori(0, TURNS) as i:
                for r in range(TURN):
                    expert(TURN * i + r)
            expert(E - 2)
            expert(E - 1, last=True)

            A(stat[:, WARM:WARM + 1], stat[:, VVAR:VVAR + 1], ACT.Sqrt).then_inc(act_step, 1)
            for n in range(TA * NH):
                act.wait_ge(y_all, n + 1)
                a, h = n // NH, n % NH
                A(EW[:, HALF * (n % 2):HALF * (n % 2) + HALF], Yb[a][h][:, :], ACT.Square,
                  accum_out=stat[:, SS3 + 2 * a + h:SS3 + 2 * a + h + 1]).then_inc(x3_sq, 1)
                act.wait_ge(x3_sq, n + 1)
            act.wait_ge(x3_var, 1)
            A(stat[:, STD3:STD3 + TA], stat[:, VAR3:VAR3 + TA], ACT.Sqrt).then_inc(x3_std, 1)
            act.wait_ge(rst_ready, 1)
            for h in range(NH):
                cs = slice(h * HALF, (h + 1) * HALF)
                act.wait_ge(xg_ready, h + 1)
                A(HV[:, 0, cs], HV[:, 0, cs], ACT.Copy, scale=stat[:, RST3:RST3 + 1]).then_inc(oa_ready, 1)

        @block.vector
        def _(dve):
            V = nc.vector
            steps = [0]

            def step(ins):
                steps[0] += 1
                ins.then_inc(dve_step, 1)
                dve.wait_ge(dve_step, steps[0])

            dve.wait_ge(rowsT_done, 1)
            V.tensor_copy(cols[:, :], B[6][:, 0:5 * KT]).then_inc(cols_ready, 1)
            dve.wait_ge(silu_done, 1)
            V.tensor_copy(cond, cT.unsqueeze(2).broadcast_to([P, KT, 32])).then_inc(cond_ready, 1)
            dve.wait_ge(x_sq, TA)
            V.tensor_scalar(stat[:, VAR:VAR + TA], stat[:, SS:SS + TA], 1.0 / D, EPS, ALU.mult, ALU.add).then_inc(x_var, 1)
            dve.wait_ge(x_std, 1)
            step(V.reciprocal(stat[:, RST:RST + TA], stat[:, STD:STD + TA]))
            for a in range(TA):
                V.tensor_scalar(HV[:, a, :], x_sb[:, a, :], stat[:, RST + a:RST + a + 1], None, ALU.mult).then_inc(xn_ready, 1)
            def add_bias(i):
                if i == 0:
                    dve.wait_ge(s_bada, 64)
                if i == 1:
                    dve.wait_ge(s_bada_rest, 64)
                dve.wait_ge(ada_used, 4 * (i + 1))
                V.tensor_tensor(mod[:, i, :], B[7][:, :], mod[:, i, :], ALU.add).then_inc(mod_ready, 1)

            add_bias(0)
            dve.wait_ge(modT_done, 1)
            mt = B[7][:, :].rearrange("p (q j r) -> p j q r", q=QW, j=4)
            step(V.tensor_copy(shm.rearrange("p (j q) -> p j q", j=NH), mt[:, 0:2, :, 0]))
            dve.wait_ge(cols_ready, 1)
            V.scalar_tensor_tensor(scm.rearrange("p (j q) -> p j q", j=NH), mt[:, 2:4, :, 0], 1.0,
                                   cols[:, 0:KT].rearrange("p (j q) -> p j q", j=NH), ALU.add, ALU.mult).then_inc(scale_ready, 1)
            dve.wait_ge(scale_ready, 1)
            dve.wait_ge(xnT_done, 1)
            for k in range(KT // 2):
                V.tensor_scalar(hf[:, k, :], B[k // 2][:, T * (k % 2):T * (k % 2) + T],
                                scm[:, k:k + 1], shm[:, k:k + 1], ALU.mult, ALU.add).then_inc(hT_dve, 1)

            def split_low(j, cs=range(SPLITS)):
                src = raw_slot(split_units[j]).rearrange("p (k n) -> p k n", k=KT)
                for c in cs:
                    dve.wait_ge(split_h, SPLITS * j + c + 1)
                    V.tensor_tensor(part_of(wl[j % 2], c), part_of(src, c), part_of(wh[j % 2], c).bitcast(f32), ALU.subtract).then_inc(split_l, 1)

            split_low(0, (0,))
            for c in range(SPLITS):
                dve.wait_ge(hh_ready, c + 1)
                V.tensor_tensor(part_of(hl, c), part_of(hf, c), part_of(hh, c).bitcast(f32), ALU.subtract).then_inc(hl_ready, 1)
            split_low(0, (1,))
            for j in range(1, 4):
                split_low(j)
            dve.wait_ge(wsT_done, 1)
            for b in range(2):
                V.tensor_copy(wsT[:, 4 * b:4 * b + 4, :], B[2 + b][:, :].rearrange("p (g t) -> p g t", t=P)).then_inc(wsT_ready, 1)
            dve.wait_ge(v_gelu, TA * NH)
            step(V.tensor_tensor(stat[:, NMU:NMU + TA], stat[:, VS:VS + 4:2], stat[:, VS + 1:VS + 4:2], ALU.add))
            V.tensor_scalar(stat[:, NMU:NMU + TA], stat[:, NMU:NMU + TA], -1.0 / D, None, ALU.mult).then_inc(v_mu, 1)
            dve.wait_ge(v_sq, TA)
            V.tensor_scalar(stat[:, VVAR:VVAR + TA], stat[:, VSS:VSS + TA], 1.0 / D, EPS, ALU.mult, ALU.add).then_inc(v_var, 1)
            dve.wait_ge(v_std, 1)
            step(V.reciprocal(stat[:, VRST:VRST + TA], stat[:, VSTD:VSTD + TA]))
            dve.wait_ge(s_lng, 16)
            for a in range(TA):
                step(V.tensor_scalar(HV[:, a, :], HV[:, a, :], stat[:, NMU + a:NMU + a + 1],
                                     stat[:, VRST + a:VRST + a + 1], ALU.add, ALU.mult))
                V.tensor_tensor(HV[:, a, :], HV[:, a, :], lng, ALU.mult).then_inc(v_ready, 1)

            def tiles(bank):
                return bank[:, :].rearrange("p (t n) -> p t n", n=T)

            def m_low(h, b):
                dve.wait_ge(mh_ready, 2 * h + b + 1)
                t2 = slice(4 * h + 2 * b, 4 * h + 2 * b + 2)
                V.tensor_tensor(ml[:, t2, :], accB[:, 2 * b:2 * b + 2, :], mh[:, t2, :].bitcast(f32), ALU.subtract).then_inc(m_ready, 1)

            dve.wait_ge(s_bs, 16)
            for h in range(NH):
                for n, s in enumerate(SECTIONS):
                    for b in range(2):
                        if b == 1 and NS * h + n < NS * NH - 1:
                            split_low(NH + NS * h + n + 2)
                        if b == 1 and s == GATE_B:
                            m_low(h, 0)
                        m = 2 * (NS * h + n) + b
                        bank = tiles(B[m % 6])
                        two = slice(2 * b, 2 * b + 2)
                        if s == SC_X:
                            dve.wait_ge(sec_done, m + 1)
                            dve.wait_ge(sec_act, act_bank(h, SC_C, b))
                            if h > 0:
                                dve.wait_ge(m_ready, 2 * h)
                            V.tensor_tensor(accA[:, two, :], accA[:, two, :], bank, ALU.mult).then_inc(sec_dve, 1)
                            dve.wait_ge(sec_dve, dve_bank(h, s, b))
                            for t in (2 * b, 2 * b + 1):
                                k = 4 * h + t
                                w = [cols[:, KT * (1 + j) + k:KT * (1 + j) + k + 1] for j in range(3)]
                                step(V.tensor_scalar(accB[:, t, :], accA[:, t, :], w[2], None, ALU.mult))
                                step(V.scalar_tensor_tensor(accB[:, t, 1:T], accA[:, t, 0:T - 1], w[1], accB[:, t, 1:T], ALU.mult, ALU.add))
                                step(V.scalar_tensor_tensor(accB[:, t, 2:T], accA[:, t, 0:T - 2], w[0], accB[:, t, 2:T], ALU.mult, ALU.add))
                        elif s == SC_B:
                            dve.wait_ge(sec_done, m + 1)
                            V.tensor_tensor(accB[:, two, :], accB[:, two, :], bank, ALU.mult).then_inc(sec_dve, 1)
                            dve.wait_ge(sec_dve, dve_bank(h, s, b))
                        elif s == GATE_A:
                            dve.wait_ge(sec_act, act_bank(h, s, b))
                            V.tensor_tensor(accB[:, two, :], accB[:, two, :], tiles(sig), ALU.mult).then_inc(sec_dve, 1)
                        elif s == U_:
                            c = 2 * h + b
                            dve.wait_ge(sp_done, c + 1)
                            bias = bs_all[:, 4 * h + 2 * b:4 * h + 2 * b + 2, :].unsqueeze(2).broadcast_to([P, 2, TA, P])
                            V.tensor_tensor(stmp.rearrange("p (t a n) -> p t a n", t=2, a=TA),
                                            B[6][:, :].rearrange("p (t a n) -> p t a n", t=2, a=TA), bias, ALU.add).then_inc(sp_used, 1)
                            dve.wait_ge(sp_used, c + 1)
                            dve.wait_ge(sec_act, act_bank(h, s, b))
                            step(V.tensor_tensor(accC[:, two, :], accC[:, two, :], tiles(stmp), ALU.mult))
                        elif s == GATE_B:
                            dve.wait_ge(sec_act, act_bank(h, s, b))
                            V.tensor_tensor(accC[:, two, :], accC[:, two, :], tiles(sig), ALU.mult).then_inc(sec_dve, 1)
                            dve.wait_ge(sec_dve, dve_bank(h, s, b))
                            V.tensor_tensor(accB[:, two, :], accB[:, two, :], accC[:, two, :], ALU.add).then_inc(m_sum, 1)
                    if s == U_:
                        add_bias(1 + h)
                m_low(h, 1)
            split_low(len(split_units) - 1)
            dve.wait_ge(fhT_done, 1)
            st_ = B[6][:, :].rearrange("p (q j r) -> p j q r", q=QW, j=4)
            V.tensor_copy(shm.rearrange("p (j q) -> p j q", j=NH), st_[:, 2:4, :, 0]).then_inc(fhT_ready, 1)
            dve.wait_ge(s_gffn, 16 * NH)
            dve.wait_ge(mod_ready, 3)
            V.scalar_tensor_tensor(mod[0:64, 2, :], mod[0:64, 2, :], 1.0, gffn, ALU.add, ALU.mult).then_inc(fs_row, 1)
            dve.wait_ge(fs_row, 1)
            for g in range(NQ):
                V.tensor_copy(gfq[CAP * g:CAP * g + CAP, :], mod[64 + 32 * (g // 2):96 + 32 * (g // 2), 2, (g % 2) * QC:(g % 2) * QC + QC]).then_inc(gf_used, 1)
            dve.wait_ge(s_bdn, 16)
            for h in range(NH):
                step(V.tensor_copy(gffn_all[0:E, :], mod[64 + 32 * h:96 + 32 * h, 2, :]))
                bh = b_dn[0:E, h * HALF:(h + 1) * HALF]
                if h < NH - 1:
                    step(V.tensor_tensor(bh, bh, gffn_all[0:E, :], ALU.mult))
                else:
                    V.tensor_tensor(bh, bh, gffn_all[0:E, :], ALU.mult).then_inc(gf_used, 1)
            for n in range(TA * NH):
                a, h = n % TA, n // TA
                cs = slice(h * HALF, (h + 1) * HALF)
                dve.wait_ge(mix_done, n + 1)
                dve.wait_ge(gm_sb, 4 * (h + 1))
                step(V.tensor_tensor(HV[:, a, cs], B[n][:, :], gate[h], ALU.mult))
                V.tensor_tensor(x_sb[:, a, cs], x_sb[:, a, cs], HV[:, a, cs], ALU.add).then_inc(x2_ready, 1)
                dve.wait_ge(x2_ready, n + 1)
                dve.wait_ge(fs_done, h + 1)
                V.tensor_tensor(HV[:, a, cs], x_sb[:, a, cs], B[6 + h][:, :], ALU.mult).then_inc(xs_ready, 1)
            dve.wait_ge(x2_sq, TA * NH)
            step(V.tensor_tensor(stat[:, VAR2:VAR2 + TA], stat[:, SS2:SS2 + 4:2], stat[:, SS2 + 1:SS2 + 4:2], ALU.add))
            V.tensor_scalar(stat[:, VAR2:VAR2 + TA], stat[:, VAR2:VAR2 + TA], 1.0 / D, EPS, ALU.mult, ALU.add).then_inc(x2_var, 1)
            dve.wait_ge(h2T_done, 3)
            V.tensor_copy(hT[:, QW:KT, 0:P], B[2][:, :].rearrange("p (k t) -> p k t", t=P)).then_inc(h2T_dve, 1)
            dve.wait_ge(x2_std, 1)
            step(V.reciprocal(stat[:, RST2:RST2 + TA], stat[:, STD2:STD2 + TA]))

            def h_norm(h, a):
                cs = slice(h * HALF, (h + 1) * HALF)
                dve.wait_ge(fh_done, h + 1)
                V.scalar_tensor_tensor(HV[:, a, cs], HV[:, a, cs], stat[:, RST2 + a:RST2 + a + 1], B[4 + h][:, :], ALU.mult, ALU.add).then_inc(h2_ready, 1)

            h_norm(0, 0)
            h_norm(0, 1)
            h_norm(1, 0)
            dve.wait_ge(shl_done, 1)
            V.tensor_tensor(shl, B[0][:, 0:E], rb, ALU.add).then_inc(shl_ready, 1)
            dve.wait_ge(shl_ready, 1)
            dve.wait_ge(lg_done, 1)
            for a in range(TA):
                step(V.scalar_tensor_tensor(logits[:, a, :], B[6][:, T + a * E:T + (a + 1) * E], stat[:, RST2 + a:RST2 + a + 1],
                                            shl, ALU.mult, ALU.add))
            for a in range(TA):
                step(V.max(top[:, a, :], logits[:, a, :]))
            V.tensor_scalar(negm, top[:, :, 0], -1.0, None, ALU.mult).then_inc(top_ready, 1)
            for a in range(TA):
                step(V.max_index(topi[:, a, :], top[:, a, :], logits[:, a, :]))
            step(V.tensor_copy(topf, topi))
            oh = onehot.rearrange("p (a j) e -> p a j e", a=TA)
            for a in range(TA):
                step(V.tensor_tensor(oh[:, a], iota[:, 0:E].unsqueeze(1).broadcast_to([P, TOP_K, E]),
                                     topf[:, a, 0:TOP_K].unsqueeze(2).broadcast_to([P, TOP_K, E]), ALU.is_equal))
            for a in range(TA):
                V.tensor_reduce(mask[:, a, :], oh[:, a].rearrange("p j e -> p e j"), AX.X, ALU.max).then_inc(mask_ready, 1)
            h_norm(1, 1)
            dve.wait_ge(exp_done, TA)
            dve.wait_ge(mask_ready, TA)
            step(V.reciprocal(esum, esum))
            step(V.tensor_tensor(topw, topw, esum.unsqueeze(2).broadcast_to([P, TA, TOP_K]), ALU.mult))
            for a in range(TA):
                step(V.tensor_tensor(oh[:, a], oh[:, a], topw[:, a, :].unsqueeze(2).broadcast_to([P, TOP_K, E]), ALU.mult))
            dve.wait_ge(rank_done, 1)
            step(V.scalar_tensor_tensor(pos[:, :, :], ranks[:, 0:TA * E].rearrange("p (a e) -> p a e", a=TA), 1.0, mask, ALU.add, ALU.mult))
            step(V.tensor_scalar(pos[:, :, :], pos[:, :, :], -1.0, None, ALU.add))

            def select(e):
                for a in range(TA):
                    V.tensor_scalar(S[:, a, :].rearrange("p (g s) -> p g s", g=NQ), iota[:, :].unsqueeze(1).broadcast_to([P, NQ, CAP]),
                                    pos[:, a, ds(e, 1)], None, ALU.is_equal).then_inc(s_ready, 1)

            def select_weighted(e):
                for a in range(TA):
                    V.tensor_scalar(Sw[:, a, :].rearrange("p (g s) -> p g s", g=NQ), iota[:, :].unsqueeze(1).broadcast_to([P, NQ, CAP]),
                                    pos[:, a, ds(e, 1)], wts[:, a, ds(e, 1)], ALU.is_equal, ALU.mult).then_inc(sw_ready, 1)

            def select_bias(e):
                V.tensor_copy(sel, ident[:, ds(4 * e, 4)].unsqueeze(2).broadcast_to([P, 4, CAP])).then_inc(sel_ready, 1)

            dve.wait_ge(c_iota, 1)
            dve.wait_ge(c_ident, 1)
            select(0)
            for a in range(TA):
                V.tensor_reduce(wts[:, a, :], oh[:, a].rearrange("p j e -> p e j"), AX.X, ALU.add).then_inc(wts_ready, 1)
            dve.wait_ge(wts_ready, TA)
            V.tensor_copy(wts4.rearrange("p a (r e) -> p a r e", e=E), wts[:, :, :].unsqueeze(2).broadcast_to([P, TA, P // E, E])).then_inc(wts_ready, 1)
            step(V.scalar_tensor_tensor(over, ranks[0:1, TA * E:TA * E + E].unsqueeze(2).broadcast_to([1, E, MAXR - 1]), 1.0 / CAP,
                                        iota[0:1, 1:MAXR].unsqueeze(1).broadcast_to([1, E, MAXR - 1]), ALU.mult, ALU.is_gt))
            step(V.tensor_reduce(nover, over, AX.X, ALU.add))
            V.tensor_copy(rounds[:, :], nover).then_inc(table_ready, 1)
            select_weighted(0)
            select_bias(0)
            dve.wait_ge(hTg_done, 1)
            V.tensor_copy(hTg, G[:, 0:QC].rearrange("p (q s) -> p q s", q=KQ)).then_inc(hTg_ready, 1)
            rnd = dve.alloc_register("dve_round")
            dve.reg_mov(rnd, 0)
            dve.wait_ge(table_ready, 1)

            def one_round(e, follower, last=False):
                n = dve.snap(rnd, min_val=0, max_val=ALL_ROUNDS)
                if not last:
                    dve.wait_ge(sw_ready, TA * n + TA)
                    V.tensor_scalar(pos[:, :, ds(e, 1)], pos[:, :, ds(e, 1)], -float(CAP), None, ALU.add).then_inc(pos_moved, 1)
                    dve.wait_ge(gathered, n + 1)
                    dve.wait_ge(pos_moved, n + 1)
                    select(follower)
                dve.wait_ge(gate_done, n + 1)
                V.tensor_scalar(gs, G[:, 0:QC], LIMIT, None, ALU.min).then_inc(gmin_ready, 1)
                dve.wait_ge(sig_ready, n + 1)
                V.tensor_tensor(gs, gs, sg, ALU.mult).then_inc(gs_ready, 1)
                dve.wait_ge(up_done, n + 1)
                V.tensor_scalar(ua, Ub[:, 0:QC], LIMIT, -LIMIT, ALU.min, ALU.max).then_inc(clip_done, 1)
                dve.wait_ge(gs_ready, n + 1)
                dve.wait_ge(clip_done, n + 1)
                V.scalar_tensor_tensor(ua, ua, 1.0, gs, ALU.add, ALU.mult).then_inc(act_ready, 1)
                if not last:
                    dve.wait_ge(hTg_done, n + 2)
                    V.tensor_copy(hTg, G[:, 0:QC].rearrange("p (q s) -> p q s", q=KQ)).then_inc(hTg_ready, 1)
                    dve.wait_ge(swT_done, n + 1)
                    select_weighted(follower)
                    if follower is not e:
                        select_bias(follower)
                dve.wait_ge(swT_ready, n + 2)
                V.tensor_scalar(ST, SwT, 0.0, None, ALU.not_equal).then_inc(st_ready, 1)
                dve.wait_ge(down_done, n + 1)
                V.scalar_tensor_tensor(yw, Db[:, 0:QC], stat[:, WSL:WSL + 1], gfq, ALU.mult, ALU.mult).then_inc(yw_ready, 1)
                dve.wait_ge(yw_ready, n + 2)
                V.tensor_copy(yp[:, 0, :], yw).then_inc(y_cut, 1)
                dve.wait_ge(y_cut, 2 * n + 1)
                V.tensor_tensor(yr, yw, yp[:, 0, :], ALU.subtract).then_inc(y_rest, 1)
                dve.wait_ge(y_rest, n + 1)
                V.tensor_copy(yp[:, 1, :], yr).then_inc(y_cut, 1)
                dve.wait_ge(y_cut, 2 * n + 2)
                for g in range(NQ):
                    rows_ = slice(CAP * g, CAP * g + CAP)
                    V.tensor_tensor(ys[2 * CAP:3 * CAP, g * QC:(g + 1) * QC], yr[rows_, :], yp[rows_, 1, :], ALU.subtract).then_inc(y_low, 1)
                dve.reg_add(rnd, rnd, 1)

            def expert(e, last=False):
                more = dve.value_load(rounds[0:1, ds(e, 1)], min_val=0, max_val=MAXR - 1)
                with dve.If(more > 0):
                    with dve.Fori(0, more):
                        one_round(e, e)
                one_round(e, e + 1, last)

            with dve.Fori(0, TURNS) as i:
                for r in range(TURN):
                    expert(TURN * i + r)
            expert(E - 2)
            expert(E - 1, last=True)

            dve.wait_ge(s_gfin, 16)
            for h in range(NH):
                dve.wait_ge(x3_sq, h + 1)
                V.tensor_tensor(HV[:, 0, h * HALF:(h + 1) * HALF], Yb[0][h][:, :], gfin[:, h * HALF:(h + 1) * HALF], ALU.mult).then_inc(xg_ready, 1)
            dve.wait_ge(x3_sq, TA * NH)
            step(V.tensor_tensor(stat[:, VAR3:VAR3 + TA], stat[:, SS3:SS3 + 4:2], stat[:, SS3 + 1:SS3 + 4:2], ALU.add))
            V.tensor_scalar(stat[:, VAR3:VAR3 + TA], stat[:, VAR3:VAR3 + TA], 1.0 / D, EPS, ALU.mult, ALU.add).then_inc(x3_var, 1)
            dve.wait_ge(x3_std, 1)
            V.reciprocal(stat[:, RST3:RST3 + TA], stat[:, STD3:STD3 + TA]).then_inc(rst_ready, 1)
            dve.wait_ge(rst_ready, 1)
            for h in range(NH):
                cs = slice(h * HALF, (h + 1) * HALF)
                V.scalar_tensor_tensor(HV[:, 1, cs], Yb[1][h][:, :], stat[:, RST3 + 1:RST3 + 2], gfin[:, cs], ALU.mult, ALU.mult).then_inc(o_ready, 1)

        @block.tensor
        def _(pe):
            M = nc.tensor.matmul
            WARM_LOAD, WARM_SPLIT, WARM_TOP, WARM_RANK, WARM_CUT = 24, 36, 24, 16, 26
            TR = nc.tensor.transpose

            def arrived(n):
                pe.wait_ge(s_slot[n % RING], 16 * (n // RING + 1))

            def split_ready(j, k):
                if k % (KT // SPLITS) == 0:
                    pe.wait_ge(split_l, SPLITS * j + k // (KT // SPLITS) + 1)

            def product(o, k, left, right):
                for n, (i, j) in enumerate(((0, 0), (0, 1), (1, 0))):
                    t = M(o, left[i], right[j], start=(k == 0 and n == 0), stop=(k == KT - 1 and n == 2))
                return t

            pe.wait_ge(c_ident, 1)
            pe.wait_ge(s_rows, 48)
            TR(B[6][:, 0:5 * KT], rows, ident[0:5 * KT, 0:5 * KT]).then_inc(rowsT_done, 1)
            def modulation(i, q):
                if q == 0 and i == 0:
                    pe.wait_ge(cond_ready, 1)
                if q == 0 and i == 1:
                    pe.wait_ge(v_gelu, TA * NH)
                if q == 0 and i == 2:
                    pe.wait_ge(mod_ready, 2)
                n = unit_no[("ada", i, q)]
                arrived(n)
                w = raw_slot(n).rearrange("p (k n) -> p k n", k=2)
                for kk in range(2):
                    for j in range(4):
                        t = M(B[7][32 * j:32 * j + 32, :], cond[:, 2 * q + kk, :], w[:, kk, HALF * j:HALF * (j + 1)],
                              start=(q + kk == 0), stop=(q == 3 and kk == 1))
                t.then_inc(ada_used, 1)

            def keep_warm(n, bank):
                for _ in range(n):
                    TR(bank[:, 0:P], ident[:, :], ident[:, :])

            modulation(0, 0)
            pe.wait_ge(xn_ready, TA)
            for k in range(KT):
                for a in range(TA):
                    c = T * (k % 2) + P * a
                    t = TR(B[k // 2][:, c:c + P], HV[:, a, k * P:(k + 1) * P], ident[:, :])
            t.then_inc(xnT_done, 1)

            for q in range(1, 4):
                keep_warm(WARM_LOAD, B[5])
                modulation(0, q)
            keep_warm(8, B[5])
            pe.wait_ge(mod_ready, 1)
            for q in range(QW):
                t = TR(B[7][:, P * q:P * q + P], mod[:, 0, P * q:P * q + P], ident[:, :])
            t.then_inc(modT_done, 1)
            keep_warm(WARM_SPLIT, B[5])
            for h in range(NH):
                if h == 0:
                    pe.wait_ge(scale_ready, 1)
                for c in range(SPLITS):
                    if h == 0:
                        pe.wait_ge(hl_ready, c + 1)
                    for a in range(TA):
                        for k in range(c * KT // SPLITS, (c + 1) * KT // SPLITS):
                            split_ready(h, k)
                            ts = slice(a * P, (a + 1) * P)
                            t = product(B[4 + 2 * h + a][:, :], k, (hh[:, k, ts], hl[:, k, ts]), (wh[h][:, k, :], wl[h][:, k, :]))
                        if c == SPLITS - 1:
                            t.then_inc(v_done, 1)

            pe.wait_ge(ws_masked, 1)
            for g in range(NG):
                t = TR(B[2 + g // 4][:, P * (g % 4):P * (g % 4) + P], ws_nat[:, g, :], ident[:, :])
            t.then_inc(wsT_done, 1)

            def spatial(c):
                if c == 0:
                    pe.wait_ge(v_ready, TA)
                    pe.wait_ge(v_gelu, TA * NH)
                else:
                    pe.wait_ge(sp_used, c)
                for g in (2 * c, 2 * c + 1):
                    for a in range(TA):
                        o = T * (g % 2) + P * a
                        t = M(B[6][:, o:o + P], HV[:, a, g * P:(g + 1) * P], wsT[:, g, :], start=True, stop=True)
                t.then_inc(sp_done, 1)

            for h in range(NH):
                for i, s in enumerate(SECTIONS):
                    j = NH + NS * h + i
                    for b in range(2):
                        if s == U_ and b == 0:
                            spatial(2 * h)
                        m = 2 * (NS * h + i) + b
                        if m == 2:
                            pe.wait_ge(wsT_ready, 2)
                        if m >= 4 and m < 6:
                            pe.wait_ge(v_gelu, m - 3)
                        if m >= 6:
                            m0 = m - 6
                            h0, s0, b0 = m0 // (2 * NS), SECTIONS[(m0 // 2) % NS], m0 % 2
                            if s0 in (SC_X, SC_B):
                                pe.wait_ge(sec_dve, dve_bank(h0, s0, b0))
                            else:
                                pe.wait_ge(sec_act, act_bank(h0, s0, b0))
                        for tt in range(2):
                            for k in range(KT):
                                split_ready(j, k)
                                cs = slice(P * (2 * b + tt), P * (2 * b + tt) + P)
                                t = product(B[m % 6][:, T * tt:T * tt + T], k, (wh[j % 2][:, k, cs], wl[j % 2][:, k, cs]),
                                            (hh[:, k, :], hl[:, k, :]))
                        t.then_inc(sec_done, 1)
                        if b == 0 and i < 4:
                            modulation(1 + h, i)
                    if s == U_:
                        spatial(2 * h + 1)

            def spread(dst, i, j, signal):
                M(dst[:, :], ident[:, 32 * j:32 * j + 1].broadcast_to([P, P]), mod[:, i, :], start=True, stop=True).then_inc(signal, 1)

            def turn_x(h, a):
                for q in range(QW):
                    k = QW * h + q
                    t = TR(B[TA * h + a][:, P * q:P * q + P], HV[:, a, k * P:(k + 1) * P], ident[:, :])
                t.then_inc(h2T_done, 1)

            def route(ks):
                for k in ks:
                    j = k % 4
                    t = M(B[6][32 * j:32 * j + 32, 0:T], rw[:, k, :], hT[:, k, :], start=(k < 4), stop=(k >= 4))
                return t

            pe.wait_ge(c_late, 1)
            pe.wait_ge(mod_ready, 2)
            pe.wait_ge(sec_act, act_bank(NH - 1, GATE_A, 1))
            for h in range(NH):
                j = NH + NS * NH + h
                for ks in (range(0, KT - 2), range(KT - 2, KT)):
                    for a in range(TA):
                        for k in ks:
                            if h + a == 0 and k % 2 == 0:
                                pe.wait_ge(m_ready, k // 2 + 1)
                            split_ready(j, k)
                            ts = slice(a * P, (a + 1) * P)
                            t = product(B[TA * h + a][:, :], k, (mh[:, k, ts], ml[:, k, ts]), (wh[j % 2][:, k, :], wl[j % 2][:, k, :]))
                        if ks[-1] == KT - 1:
                            t.then_inc(mix_done, 1)
                        if h == NH - 1 and a == 0 and ks[0] == 0:
                            pe.wait_ge(fs_row, 1)
                            pe.wait_ge(fhT_ready, 1)
                            for i in range(NH):
                                spread(B[6 + i], 2, i, fs_done)
                    if h == 0 and ks[0] == 0:
                        pe.wait_ge(sec_act, act_bank(NH - 1, GATE_B, 1))
                        pe.wait_ge(sp_used, NG // 2)
                        for q in range(QW):
                            t = TR(B[6][:, P * q:P * q + P], mod[:, 1, P * q:P * q + P], ident[:, :])
                        t.then_inc(fhT_done, 1)
                    if h == NH - 1 and ks[0] == 0:
                        pe.wait_ge(xs_ready, TA)
                        for a in range(TA):
                            turn_x(0, a)
                if h == 0:
                    for i in range(NH):
                        spread(B[4 + i], 1, 2 + i, fh_done)
            pe.wait_ge(h2T_act, 2)
            pe.wait_ge(s_rw, 32)
            route(range(0, 4))
            for k in range(KT):
                t = M(B[0][:, 0:E], shm[:, k:k + 1].broadcast_to([P, P]), rw[:, k, :], start=(k == 0), stop=(k == KT - 1))
            t.then_inc(shl_done, 1)
            for a in range(TA):
                pe.wait_ge(xs_ready, TA + a + 1)
                turn_x(1, a)
            pe.wait_ge(h2T_dve, 1)
            pe.wait_ge(h2T_act, 3)
            route(range(4, 8)).then_inc(part_done, 1)
            keep_warm(5, B[1])
            pe.wait_ge(part_ready, 1)
            for a in range(TA):
                t = M(B[6][:, T + a * E:T + (a + 1) * E], part[:, a * P:(a + 1) * P], stack, start=True, stop=True)
            t.then_inc(lg_done, 1)
            keep_warm(WARM_TOP, B[1])
            pe.wait_ge(mask_ready, TA)
            pe.wait_ge(h2_ready, TA)
            M(ranks[:, 0:E], below, mask[:, 0, :], start=True, stop=True)
            M(ranks[:, E:2 * E], below, mask[:, 1, :], start=True, stop=False)
            M(ranks[:, E:2 * E], ones, mask[:, 0, :], start=False, stop=True)
            M(ranks[:, 2 * E:3 * E], ones, mask[:, 0, :], start=True, stop=False)
            M(ranks[:, 2 * E:3 * E], ones, mask[:, 1, :], start=False, stop=True).then_inc(rank_done, 1)

            def gather():
                for a in range(TA):
                    for g in range(NQ):
                        t = M(Db[CAP * g:CAP * g + CAP, 0:QC], S[:, a, CAP * g:CAP * g + CAP], HV[:, a, g * QC:(g + 1) * QC],
                              start=(a == 0), stop=(a == TA - 1))
                t.then_inc(gathered, 1)

            def turn(dst, src, signal):
                for q in range(KQ):
                    t = TR(dst[:, P * q:P * q + P], src[:, P * q:P * q + P], ident[:, :])
                t.then_inc(signal, 1)

            def open_sum(a, h):
                M(Yb[a][h][:, :], wT[:, a * P:(a + 1) * P], b_dn[:, h * HALF:(h + 1) * HALF],
                  start=True, stop=True, skip_group_check=True)

            keep_warm(WARM_RANK, B[1])
            pe.wait_ge(s_ready, TA)
            pe.wait_ge(h2_ready, TA * NH)
            gather()
            pe.wait_ge(wts_ready, TA + 1)
            for a in range(TA):
                t = TR(B[7][:, a * P:(a + 1) * P], wts4[:, a, :], ident[:, :])
            t.then_inc(wT_done, 1)
            pe.wait_ge(hg_ready, 1)
            pe.wait_ge(table_ready, 1)
            turn(G, hg, hTg_done)
            pe.wait_ge(wT_ready, 1)
            pe.wait_ge(gf_used, NQ + 1)
            pe.wait_ge(dn_zero, 1)
            for a in range(TA):
                for h in range(NH):
                    open_sum(a, h)
            pe.wait_ge(y_zero, 2)
            pe.wait_ge(s_bgu, 16)
            rnd = pe.alloc_register("pe_round")
            pe.reg_mov(rnd, 0)

            def stream(dst, src, b, uses, first, done):
                for k in range(KT):
                    if k % 2 == 0:
                        pe.wait_ge(s_block[b % PAIRS][k // 2], 16 * uses)
                    for g in range(NQ):
                        t = M(dst[CAP * g:CAP * g + CAP, 0:QC], src[:, k % KQ, CAP * (k // KQ):CAP * (k // KQ) + CAP],
                              w_half(block_slot(b), k)[:, g * QC:(g + 1) * QC], start=(first and k == 0), stop=(k == KT - 1))
                    if done and k % 2 == 1 and k < KT - 1:
                        t.then_inc(released, 1)
                return t

            def bias(dst, j0):
                ts = [M(dst[CAP * g:CAP * g + CAP, 0:QC], sel[:, j0 + g // 2, :], b_gu[:, QC * (g % 2):QC * (g % 2) + QC],
                        start=True, stop=False) for g in range(NQ)]
                return ts[0]

            def scatter(signal=None):
                for a in range(TA):
                    for h in range(NH):
                        t = M(Yb[a][h][:, :], ST[0:PARTS * CAP, a * P:(a + 1) * P], ys[:, h * HALF:(h + 1) * HALF],
                              start=False, stop=True, skip_group_check=True)
                        if signal is not None:
                            t.then_inc(signal, 1)
                return t

            def wait_outputs(n):
                pe.wait_ge(y_moved, 2 * NQ * n + 2 * NQ)
                pe.wait_ge(y_low, NQ * n + NQ)
                pe.wait_ge(st_ready, n + 1)

            def one_round(e, b, turns, done, last=False):
                n = pe.snap(rnd, min_val=0, max_val=ALL_ROUNDS)
                uses = [3 * turns + block_uses(b + i) for i in range(3)]
                pe.wait_ge(sel_ready, e + 1)
                pe.wait_ge(hTg_ready, n + 1)
                bias(G, 0)
                stream(G, hTg, b + GATE, uses[GATE], False, done).then_inc(gate_done, 1)
                pe.wait_ge(swT_ready, n + 1)
                t = bias(Ub, 2)
                if done:
                    t.then_inc(released, 1)
                stream(Ub, hTg, b + UP, uses[UP], False, done).then_inc(up_done, 1)
                if not last:
                    pe.wait_ge(yw_ready, n + 1)
                    pe.wait_ge(s_ready, TA * n + 2 * TA)
                    gather()
                wait_outputs(n)
                t = scatter()
                if done:
                    t.then_inc(released, 1)
                if last:
                    for a in range(TA):
                        for h in range(NH):
                            M(Yb[a][h][:, :], ident[:, :], x_sb[:, a, h * HALF:(h + 1) * HALF],
                              start=False, stop=True, skip_group_check=True)
                pe.wait_ge(act_ready, n + 1)
                turn(Xb, ua, actT_done)
                if not last:
                    pe.wait_ge(hg_ready, n + 2)
                    turn(G, hg, hTg_done)
                pe.wait_ge(sw_ready, TA * n + TA)
                for a in range(TA):
                    t = TR(Ub[:, a * P:(a + 1) * P], Sw[:, a, :], ident[:, :])
                t.then_inc(swT_done, 1)
                pe.wait_ge(actT_ready, n + 1)
                stream(Db, actT, b + DOWN, uses[DOWN], True, done).then_inc(down_done, 1)
                if done:
                    pe.wait_ge(down_done, n + 1)
                    pe.nop().then_inc(released, 1)
                pe.reg_add(rnd, rnd, 1)

            def expert(e, b, turns, last=False):
                more = pe.value_load(rounds[0:1, ds(e, 1)], min_val=0, max_val=MAXR - 1)
                with pe.If(more > 0):
                    with pe.Fori(0, more):
                        one_round(e, b, turns, False)
                one_round(e, b, turns, True, last)

            with pe.Fori(0, TURNS) as i:
                for r in range(TURN):
                    expert(TURN * i + r, 3 * r, i)
            expert(E - 2, 0, TURNS)
            expert(E - 1, 3, TURNS, last=True)
            n = pe.snap(rnd, min_val=0, max_val=ALL_ROUNDS)
            pe.wait_ge(swT_ready, n + 1)
            keep_warm(WARM_CUT, G)
            wait_outputs(n)
            scatter(y_all)


_INS = ["x", "c", "w_ada", "b_ada", "norm_mix_g", "w_in", "conv_w", "w_spatial", "b_spatial", "ln_v_g",
        "w_out", "norm_ffn_g", "router_w", "router_b", "w_gate_up", "b_gate_up", "w_down", "b_down",
        "final_norm_g"]


def kernel(**inputs):
    import numpy as _np
    import concourse.bacc as _bacc
    from concourse import mybir as _mybir
    from concourse.bass_utils import run_bass_kernel_spmd as _run

    nc = _bacc.Bacc("TRN2", target_bir_lowering=False, num_devices=1)
    arrays, args = {}, []
    for name in _INS:
        a = _np.ascontiguousarray(inputs[name])
        arrays[f"in_{name}_dram"] = a
        args.append(nc.dram_tensor(f"in_{name}_dram", a.shape, _mybir.dt.from_np(a.dtype), kind="ExternalInput").ap())
    shape = tuple(inputs["x"].shape)
    args.append(nc.dram_tensor("out_0_dram", shape, _mybir.dt.float32, kind="ExternalOutput").ap())
    hybrid_trunk(nc, *args)
    r = _run(nc, [arrays], core_ids=[0])
    return r.results[0]["out_0_dram"]
```
